# Optimizing a Trainium2 kernel written in Bass

```python
import jax, jax.numpy as jnp
from jax import lax
import numpy as np

D_MODEL = 1024
BATCH = 1
SEQ = 512
DEPTH = 1

N_META = 16
CONV_DIM = 512
CONV_WIDTH = 31
RET_HEADS = 4
RET_DK = 128
RET_DV = 256
RET_CHUNK = 128
ROPE_BASE = 10000.0
PEER_HEADS = 8
PEER_NKEYS = 128
PEER_NEXPERTS = PEER_NKEYS * PEER_NKEYS
PEER_DKEY = 256
PEER_TOPK = 16
PEER_BLOCK = 256
EPS = 1e-6

QK_W = RET_HEADS * RET_DK
V_W = RET_HEADS * RET_DV
IN_COLS = 2 * CONV_DIM + 2 * QK_W + 2 * V_W + 2 * D_MODEL
SPLIT_POINTS = (
    CONV_DIM,
    2 * CONV_DIM,
    2 * CONV_DIM + QK_W,
    2 * CONV_DIM + 2 * QK_W,
    2 * CONV_DIM + 2 * QK_W + V_W,
    2 * CONV_DIM + 2 * QK_W + 2 * V_W,
    2 * CONV_DIM + 2 * QK_W + 2 * V_W + D_MODEL,
)

kernel_name = "hybrid_conv_retention_peer_block"

def rmsnorm(x, g):
    xf = x.astype(jnp.float32)
    y = xf * lax.rsqrt(jnp.mean(xf * xf, axis=-1, keepdims=True) + EPS)
    return (y * g.astype(jnp.float32)).astype(x.dtype)

def layernorm(x, g, b):
    xf = x.astype(jnp.float32)
    mu = jnp.mean(xf, axis=-1, keepdims=True)
    var = jnp.mean(jnp.square(xf - mu), axis=-1, keepdims=True)
    y = (xf - mu) * lax.rsqrt(var + EPS)
    return (y * g.astype(jnp.float32) + b.astype(jnp.float32)).astype(x.dtype)

def rotary(t, pos):
    half = t.shape[-1] // 2
    freqs = ROPE_BASE ** (-jnp.arange(half, dtype=jnp.float32) / half)
    ang = pos[:, None] * freqs[None, :]
    cos = jnp.cos(ang)[None, :, None, :]
    sin = jnp.sin(ang)[None, :, None, :]
    t1, t2 = t[..., :half], t[..., half:]
    return jnp.concatenate([t1 * cos - t2 * sin, t1 * sin + t2 * cos], axis=-1)

def conv_module(a, b, dw_w, dw_b, ln_g, ln_b, proj_w):
    h = a * jax.nn.sigmoid(b)
    h = lax.conv_general_dilated(
        h, dw_w[:, None, :].astype(h.dtype), window_strides=(1,),
        padding=[(CONV_WIDTH - 1, 0)], dimension_numbers=("NWC", "WIO", "NWC"),
        feature_group_count=CONV_DIM) + dw_b
    h = jax.nn.silu(layernorm(h, ln_g, ln_b))
    return h @ proj_w

def retention(q, k, v, g, proj_w):
    B, L = q.shape[0], q.shape[1]
    out_dtype = v.dtype
    pos = jnp.arange(L, dtype=jnp.float32)
    q = rotary(q.astype(jnp.float32), pos)
    k = rotary(k.astype(jnp.float32), pos) * (RET_DK ** -0.5)
    v = v.astype(jnp.float32)
    pad = (-L) % RET_CHUNK
    Lp = L + pad
    n_chunks = Lp // RET_CHUNK

    def to_chunks(t):
        t = jnp.pad(t, ((0, 0), (pad, 0), (0, 0), (0, 0)))
        return t.reshape(B, n_chunks, RET_CHUNK, RET_HEADS, t.shape[-1]).transpose(1, 0, 3, 2, 4)

    qc, kc, vc = to_chunks(q), to_chunks(k), to_chunks(v)

    log_gamma = jnp.log(1.0 - 2.0 ** (-5.0 - jnp.arange(RET_HEADS, dtype=jnp.float32)))
    i = jnp.arange(RET_CHUNK, dtype=jnp.float32)
    rel = i[:, None] - i[None, :]
    decay_mask = jnp.where(rel >= 0, jnp.exp(log_gamma[:, None, None] * jnp.maximum(rel, 0.0)), 0.0)
    xi = jnp.exp(log_gamma[:, None] * (i[None, :] + 1.0))
    zeta = jnp.exp(log_gamma[:, None] * (RET_CHUNK - 1.0 - i[None, :]))
    gamma_c = jnp.exp(log_gamma * RET_CHUNK)

    def step(state, xs):
        qb, kb, vb = xs
        scores = jnp.einsum("bhid,bhjd->bhij", qb, kb) * decay_mask
        inner = jnp.einsum("bhij,bhjv->bhiv", scores, vb)
        cross = jnp.einsum("bhid,bhdv->bhiv", qb, state) * xi[None, :, :, None]
        state = state * gamma_c[None, :, None, None] + jnp.einsum(
            "bhjd,bhjv->bhdv", kb * zeta[None, :, :, None], vb)
        return state, inner + cross

    state0 = jnp.zeros((B, RET_HEADS, RET_DK, RET_DV), jnp.float32)
    _, o = lax.scan(step, state0, (qc, kc, vc))
    o = o.transpose(1, 0, 3, 2, 4).reshape(B, Lp, RET_HEADS, RET_DV)[:, pad:]
    o = o * lax.rsqrt(jnp.mean(o * o, axis=-1, keepdims=True) + EPS)
    o = o.reshape(B, L, V_W) * jax.nn.silu(g.astype(jnp.float32))
    return o.astype(out_dtype) @ proj_w

def peer(xn, w_q, sub_keys, u_tab, v_tab):
    B, L, D = xn.shape
    T = B * L
    n_blocks = -(-T // PEER_BLOCK)
    t = jnp.pad(xn.reshape(T, D), ((0, n_blocks * PEER_BLOCK - T), (0, 0)))
    blocks = t.reshape(n_blocks, PEER_BLOCK, D)

    def block_fn(xb):
        q = (xb @ w_q).reshape(PEER_BLOCK, PEER_HEADS, 2, PEER_DKEY // 2)
        s = jnp.einsum("thpd,hpkd->thpk", q, sub_keys)
        s_top, i_top = lax.top_k(s, PEER_TOPK)
        cand = s_top[:, :, 0, :, None] + s_top[:, :, 1, None, :]
        c_top, c_idx = lax.top_k(cand.reshape(PEER_BLOCK, PEER_HEADS, PEER_TOPK * PEER_TOPK), PEER_TOPK)
        ia = jnp.take_along_axis(i_top[:, :, 0], c_idx // PEER_TOPK, axis=-1)
        ib = jnp.take_along_axis(i_top[:, :, 1], c_idx % PEER_TOPK, axis=-1)
        expert = ia * PEER_NKEYS + ib
        gate = jax.nn.softmax(c_top.astype(jnp.float32), axis=-1)
        u = jnp.take(u_tab, expert, axis=0)
        act = jax.nn.gelu(jnp.einsum("thkd,td->thk", u, xb).astype(jnp.float32))
        w = (gate * act).astype(xb.dtype)
        return jnp.einsum("thk,thkd->td", w, jnp.take(v_tab, expert, axis=0))

    out = lax.map(block_fn, blocks).reshape(n_blocks * PEER_BLOCK, D)[:T]
    return out.reshape(B, L, D)

def setup_inputs(seed: int = 0) -> dict:
    key = jax.random.key(seed)
    ks = jax.random.split(key, 20)
    f32 = jnp.float32
    nrm = lambda k, shape, s: jax.random.normal(k, shape, f32) * s
    return {
        "x": nrm(ks[0], (BATCH, SEQ, D_MODEL), 1.0),
        "meta_tokens": nrm(ks[1], (N_META, D_MODEL), 1.0),
        "norm_mix_g": 1.0 + nrm(ks[2], (DEPTH, D_MODEL), 0.01),
        "w_in": nrm(ks[3], (DEPTH, D_MODEL, IN_COLS), D_MODEL ** -0.5),
        "conv_dw_w": nrm(ks[4], (DEPTH, CONV_WIDTH, CONV_DIM), CONV_WIDTH ** -0.5),
        "conv_dw_b": nrm(ks[5], (DEPTH, CONV_DIM), 0.01),
        "conv_ln_g": 1.0 + nrm(ks[6], (DEPTH, CONV_DIM), 0.01),
        "conv_ln_b": nrm(ks[7], (DEPTH, CONV_DIM), 0.01),
        "conv_proj_w": nrm(ks[8], (DEPTH, CONV_DIM, D_MODEL), CONV_DIM ** -0.5),
        "ret_proj_w": nrm(ks[9], (DEPTH, V_W, D_MODEL), V_W ** -0.5),
        "w_out": nrm(ks[10], (DEPTH, D_MODEL, D_MODEL), D_MODEL ** -0.5),
        "norm_ffn_g": 1.0 + nrm(ks[11], (DEPTH, D_MODEL), 0.01),
        "peer_w_q": nrm(ks[12], (DEPTH, D_MODEL, PEER_HEADS * PEER_DKEY), D_MODEL ** -0.5),
        "peer_sub_keys": nrm(ks[13], (DEPTH, PEER_HEADS, 2, PEER_NKEYS, PEER_DKEY // 2), (PEER_DKEY // 2) ** -0.5),
        "peer_u": nrm(ks[14], (DEPTH, PEER_NEXPERTS, D_MODEL), D_MODEL ** -0.5),
        "peer_v": nrm(ks[15], (DEPTH, PEER_NEXPERTS, D_MODEL), 0.5),
        "norm_final_g": 1.0 + nrm(ks[16], (D_MODEL,), 0.01),
    }

def reference(x, meta_tokens, norm_mix_g, w_in, conv_dw_w, conv_dw_b, conv_ln_g, conv_ln_b,
              conv_proj_w, ret_proj_w, w_out, norm_ffn_g, peer_w_q, peer_sub_keys,
              peer_u, peer_v, norm_final_g):
    B = x.shape[0]
    meta = jnp.broadcast_to(meta_tokens[None].astype(x.dtype), (B, N_META, D_MODEL))
    h = jnp.concatenate([meta, x], axis=1)
    L = h.shape[1]
    for l in range(DEPTH):
        xn = rmsnorm(h, norm_mix_g[l])
        z = xn @ w_in[l]
        a, b, q, k, v, g, gate_c, gate_r = jnp.split(z, SPLIT_POINTS, axis=-1)
        conv_out = conv_module(a, b, conv_dw_w[l], conv_dw_b[l], conv_ln_g[l], conv_ln_b[l], conv_proj_w[l])
        ret_out = retention(q.reshape(B, L, RET_HEADS, RET_DK), k.reshape(B, L, RET_HEADS, RET_DK),
                            v.reshape(B, L, RET_HEADS, RET_DV), g, ret_proj_w[l])
        merged = jax.nn.sigmoid(gate_c) * conv_out + jax.nn.sigmoid(gate_r) * ret_out
        h = h + merged @ w_out[l]
        h = h + peer(rmsnorm(h, norm_ffn_g[l]), peer_w_q[l], peer_sub_keys[l], peer_u[l], peer_v[l])
    y = rmsnorm(h, norm_final_g)
    return y[:, N_META:]


_drawn_inputs = setup_inputs


def setup_inputs(seed=0):
    import zlib

    import numpy as np

    out = dict(_drawn_inputs(seed))
    spreads = {}
    factors = {'conv_dw_b': 7.789,
     'conv_ln_g': 53.616,
     'conv_ln_b': 56.031,
     'norm_final_g': 187.903,
     'norm_mix_g': 8.53,
     'norm_ffn_g': 21.161}
    for name, (base, spread) in spreads.items():
        noise = np.random.default_rng([zlib.crc32(name.encode()), seed]).standard_normal(out[name].shape)
        drawn = base * np.exp(spread * noise) if base else spread * noise
        out[name] = __import__('jax').numpy.asarray(drawn.astype(out[name].dtype))
    for name, factor in factors.items():
        out[name] = (out[name] * factor).astype(out[name].dtype)
    return out
```

```python
from contextlib import ExitStack

import numpy as np

import concourse.bass as bass
from concourse import mybir

P = 128
D = 1024
T = 512
META = 16
L = META + T
NT = T // P
KD = D // P
CONV = 512
TAPS = 31
CT = CONV // P
HEADS = 4
DV = 256
PAD = TAPS - 1 - META
N = 512
HALF = L // 2
PH = 8
NK = 128
TOP = 16
GROUPS = NT * PH
SLOTS = 8
BANKS = 8
EPS = 1e-6
LOWEST = -3.4e38

f32 = mybir.dt.float32
bf16 = mybir.dt.bfloat16
u32 = mybir.dt.uint32
ALU = mybir.AluOpType
ACT = mybir.ActivationFunctionType
AX = mybir.AxisListType


def plan_banks():
    units = [("xT", 0, 0, "act")] + [("xT", t, i, "act") for t in range(1, NT + 1) for i in range(2)]
    units += [("b", c, i, "act") for c in range(CT) for i in range(2)]
    units += [("a", c, i, "dve") for c in range(CT) for i in range(2)]
    units += [("q", h, 0, "dve") for h in range(HEADS)]
    units += [("k", h, i, "dve") for h in range(HEADS) for i in range(2)]
    units += [("v", n, t, "act") for n in range(2) for t in range(NT + 1)]
    units += [("g", n, t, "dve") for n in range(2) for t in range(NT)]
    for h in range(HEADS + 1):
        if h < HEADS:
            units += [("sc", h, j, "dve") for j in range(NT + 1)]
        if h > 0:
            units += [("pv", h - 1, i, "dve") for i in range(NT)]
    units += [("gc", 0, t, "act") for t in range(NT)]
    units += [("mean", 0, 0, "dve")]
    units += [("gc", 1, t, "act") for t in range(NT)]
    units += [("gr", 0, t, "act") for t in range(NT)]
    units += [("var", 0, 0, "dve")]
    units += [("gr", 1, t, "act") for t in range(NT)]
    units += [("oT", t, i, "act") for t in range(NT) for i in range(2)]
    units += [("cp", n, t, "dve") for n in range(2) for t in range(NT)]
    units += [("rp", n, t, "dve") for n in range(2) for t in range(NT)]
    units += [("mT", t, i, "act") for t in range(NT) for i in range(2)]
    units += [("wo", n, t, "dve") for n in range(2) for t in range(NT)]
    units += [("zT", t, i, "act") for t in range(NT) for i in range(2)]
    for hp in range(2 * PH + 1):
        if hp < 2 * PH:
            units += [("wq", hp, 0, "act")]
        if hp > 0:
            units += [("s", hp - 1, 0, "act")]
    at, nth, count = {}, [], {"act": 0, "dve": 0}
    for u, (stage, i, j, owner) in enumerate(units):
        count[owner] += 1
        at[stage, i, j] = u
        nth.append((owner, count[owner]))
    return at, nth


def weight_chunks():
    order = [("in", n) for n in (1, 0, 2, 3, 4, 5, 6, 7, 8, 9, 10, 11)]
    return order + [("conv", 0), ("ret", 0), ("ret", 1), ("out", 0), ("out", 1)] + [("q", n) for n in range(4)]


def block_kernel(nc, x, meta, w_in, conv_w, conv_b, ln_g, ln_b, conv_proj, ret_proj, w_out, mix_g,
                 ffn_g, final_g, peer_wq, keys, peer_u, peer_v, cosine, sine, decay, identity, out):
    at, nth = plan_banks()
    chunks = weight_chunks()
    chunk_at = {c: n for n, c in enumerate(chunks)}
    WSLOTS = 2

    ctx = ExitStack()
    with ctx:
        def sem(name):
            return ctx.enter_context(nc.semaphore(name))

        words = {}
        total = 0

        def region(name, size):
            nonlocal total
            words[name] = (total, size)
            total += size

        region("LTA", KD * L)
        region("CV", CT * T)
        region("DK", HEADS * L)
        region("SPAD", (GROUPS + 1) * 2 * NK - (KD * L + CT * T + HEADS * L))
        region("X", NT * D)
        region("BIGA", NT * D)
        region("V", NT * D + D)
        region("R1", 2 * NT * D)
        region("LTB", NT * D)
        region("W", WSLOTS * KD * N)
        region("XN2", NT * D)
        region("MT", D)
        region("G1", D)
        region("G2", D)
        region("TMP", 4 * N)
        region("KEY", 2 * NK)
        region("IDENT", P)
        region("ONES", 2 * P)
        region("SMALL", 4 * 34 + 64)
        assert total * 4 <= 212800, total * 4
        arena = ctx.enter_context(nc.sbuf_tensor("arena", [P, total], f32))

        def view(name, offset=0, size=None):
            start, full = words[name]
            return arena[:, start + offset:start + offset + (full - offset if size is None else size)]

        xT = view("LTA").rearrange("p (k t) -> p k t", k=KD)
        mT = view("LTA", 0, KD * T).rearrange("p (k t) -> p k t", k=KD)
        cv = view("CV").rearrange("p (c t) -> p c t", c=CT)
        dk = view("DK").rearrange("p (h t) -> p h t", h=HEADS)
        start_s = words["LTA"][0]
        scores = arena[:, start_s:start_s + (GROUPS + 1) * 2 * NK]
        scores_t = scores[:, 0:GROUPS * 2 * NK].rearrange("p (t s k) -> p t s k", t=NT, s=2 * PH)
        X = view("X").rearrange("p (t d) -> p t d", t=NT)
        big_a = view("BIGA").rearrange("p (t d) -> p t d", t=NT)
        v_x = view("V", 0, NT * D).rearrange("p (t d) -> p t d", t=NT)
        v_meta = view("V", NT * D, D)
        q_t = view("R1", 0, HEADS * T).rearrange("p (h t) -> p h t", h=HEADS)
        k_t = view("R1", HEADS * T, HEADS * L).rearrange("p (h t) -> p h t", h=HEADS)
        TRI = T + T + 384 + 256 + 128
        p_at = [0, T, 2 * T, 2 * T + 384, 2 * T + 640]
        p_buf = view("R1", HEADS * (T + L), 2 * TRI).rearrange("p (b n) -> p b n", b=2)
        sig_b = view("R1", HEADS * (T + L), CT * L).rearrange("p (c t) -> p c t", c=CT)
        big_b = view("R1", 0, NT * D).rearrange("p (t d) -> p t d", t=NT)
        big_c = view("R1", NT * D, NT * D).rearrange("p (t d) -> p t d", t=NT)
        hb = view("LTB", 0, CT * (PAD + L)).rearrange("p (c t) -> p c t", c=CT)
        oT = view("LTB").rearrange("p (k t) -> p k t", k=KD)
        W = view("W").rearrange("p (w n) -> p w n", w=WSLOTS)
        xn2 = view("XN2").rearrange("p (t d) -> p t d", t=NT)
        cosv, sinv = view("XN2", 0, L), view("XN2", L, L)
        squares = view("XN2", 2 * L, CT * T).rearrange("p (c t) -> p c t", c=CT)
        meta_t = view("MT")
        g1, g2 = view("G1"), view("G2")
        tmp = view("TMP").rearrange("p (b n) -> p b n", b=4)
        key_t = view("KEY").rearrange("p (b n) -> p b n", b=2)
        ident, ones = view("IDENT"), view("ONES", 0, P)
        cw = view("SMALL", 0, CT * TAPS).rearrange("p (c w) -> p c w", c=CT)
        cb, lg, lb = (view("SMALL", CT * TAPS + i * CT, CT) for i in range(3))
        stat, eps = view("SMALL", 4 * 34, 60), view("SMALL", 4 * 34 + 60, 1)
        q_top = view("TMP", 0, 2 * N).rearrange("p (b n) -> p b n", b=2)
        ring0 = words["BIGA"][0]
        u_ring = arena[:, ring0:ring0 + SLOTS * D].rearrange("p (s d) -> p s d", s=SLOTS)
        v_ring = arena[:, ring0 + SLOTS * D:ring0 + 2 * SLOTS * D].rearrange("p (s d) -> p s d", s=SLOTS)
        diag = arena[:, ring0 + 2 * SLOTS * D:ring0 + 2 * SLOTS * D + SLOTS * P].rearrange("p (s n) -> p s n", s=SLOTS)
        x_cur = view("G1")
        junk = view("MT", 0, N).bitcast(bf16)
        small, used = {}, 0

        def little(name, size):
            nonlocal used
            small[name] = view("TMP", 2 * N + used, size)
            used += size

        for name, size in (("pair", 2 * NK), ("rest", NK), ("vals", 2 * TOP), ("keyf", 2 * TOP), ("top", TOP),
                           ("posf", 2 * TOP), ("chosen", 2 * TOP), ("act", TOP), ("arg", TOP), ("th", TOP),
                           ("gate", TOP), ("w", 2 * TOP), ("soft", 8), ("iota", TOP)):
            little(name, size)
        pair_scores = view("MT", N, TOP * TOP)
        hot = view("MT", N + TOP * TOP, TOP * TOP)
        rest2 = view("G2", 0, TOP * TOP)
        zeros = view("ONES", P, P)
        soft, weights = small["soft"], small["w"]
        X_flat, xn2_flat = view("X"), view("XN2")
        tmp_wide = view("TMP", 0, 2 * N)
        final_sq = junk
        little("expd", TOP)
        gate_exp = small["expd"]
        little("ids", 2 * TOP)
        little("pos", 3 * TOP)
        little("experts", 2 * TOP)
        ids = small["ids"].bitcast(u32)
        pos = small["pos"].bitcast(u32)
        experts = small["experts"].bitcast(u32)
        assert used <= 2 * N, used

        banks = [ctx.enter_context(nc.psum_tensor(f"bank{i}", [P, N], f32))[:, :] for i in range(BANKS)]

        x_in = sem("x_in")
        tables_in = sem("tables_in")
        ident_in, gains_in = sem("ident_in"), sem("gains_in")
        w_in_slot = [sem(f"w_in_slot{i}") for i in range(WSLOTS)]
        key_in = [sem(f"key_in{i}") for i in range(2)]
        unit_done = sem("unit_done")
        emptied = {"act": sem("act_emptied"), "dve": sem("dve_emptied")}
        dve_step, fin_step = sem("dve_step"), sem("fin_step")
        ssq_ready, normed = sem("ssq_ready"), sem("normed")
        consts_set = sem("consts_set")
        swapped, swap_used = sem("swapped"), sem("swap_used")
        gsig_ready, gsig_used = sem("gsig_ready"), sem("gsig_used")
        p_ready = sem("p_ready")
        pv_ssq, og_done = sem("pv_ssq"), sem("og_done")
        conv_done, centered, squared, scaled, conv_sig, conv_act = (
            sem(n) for n in ("conv_done", "centered", "squared", "scaled", "conv_sig", "conv_act"))
        merged, h_ready, h_ssq, xn2_ready = (sem(n) for n in ("merged", "h_ready", "h_ssq", "xn2_ready"))
        x_again = sem("x_again")
        scores_ready = sem("scores_ready")
        top_ready, soft_ready = sem("top_ready"), sem("soft_ready")
        idx_ready, arg_ready, tanh_ready, w_ready = (sem(n) for n in ("idx_ready", "arg_ready", "tanh_ready", "w_ready"))
        u_in = [sem(f"u_in{i}") for i in range(SLOTS)]
        v_in = [sem(f"v_in{i}") for i in range(SLOTS)]
        u_used, v_used = sem("u_used"), sem("v_used")
        diag_ready = sem("diag_ready")
        y_done, y_copied = sem("y_done"), sem("y_copied")
        slots_found = sem("slots_found")
        act_step, root_ready = sem("act_step"), sem("root_ready")
        group_step, tile_set, iota_set = sem("group_step"), sem("tile_set"), sem("iota_set")
        fin_ssq, y_out, g_final_in, stored = (sem(n) for n in ("fin_ssq", "y_out", "g_final_in", "stored"))

        block = ctx.enter_context(nc.Block())

        def wait_unit(eng, stage, i, j=0):
            u = at[stage, i, j]
            eng.wait_ge(unit_done, u + 1)
            return banks[u % BANKS]

        def wait_emptied(eng, stage, i, j=0):
            owner, n = nth[at[stage, i, j]]
            eng.wait_ge(emptied[owner], n)

        def wait_chunk(eng, name, n):
            c = chunk_at[name, n]
            eng.wait_ge(w_in_slot[c % WSLOTS], 16 * (c // WSLOTS + 1))
            return W[:, c % WSLOTS, :].rearrange("p (k n) -> p k n", k=CT if name == "conv" else KD)

        last_of = dict(zip(chunks, [("b", 3, 1), ("a", 3, 1), ("q", 3, 0), ("k", 3, 1), ("v", 0, NT), ("v", 1, NT),
                                    ("g", 0, 3), ("g", 1, 3), ("gc", 0, 3), ("gc", 1, 3), ("gr", 0, 3), ("gr", 1, 3),
                                    ("cp", 1, 3), ("rp", 0, 3), ("rp", 1, 3), ("wo", 0, 3), ("wo", 1, 3)]
                            + [("wq", 4 * n + 3, 0) for n in range(4)]))
        spans = [(0, HALF), (HALF, L)]

        @block.sync
        def _(sp):
            sp.dma_start(meta_t[0:META, :], meta).then_inc(x_in, 16)
            sp.dma_start(X, x.rearrange("(t p) d -> p t d", p=P)).then_inc(x_in, 16)
            sp.dma_start(g1, mix_g.partition_broadcast(P)).then_inc(gains_in, 16)
            sp.dma_start(ident, identity).then_inc(ident_in, 16)

            def load_chunk(c):
                name, n = chunks[c]
                src = {"in": w_in, "conv": conv_proj, "ret": ret_proj, "out": w_out, "q": peer_wq}[name]
                if c >= WSLOTS:
                    wait_unit(sp, *last_of[chunks[c - WSLOTS]])
                dst = W[:, c % WSLOTS, :]
                if name == "conv":
                    dst, src = dst.rearrange("p (k n) -> p k n", k=CT), src
                else:
                    dst, src = dst.rearrange("p (k n) -> p k n", k=KD), src[:, n * N:(n + 1) * N]
                sp.dma_start(dst, src.rearrange("(k p) n -> p k n", p=P)).then_inc(w_in_slot[c % WSLOTS], 16)

            load_chunk(0)
            for dst, src in ((cosv, cosine), (sinv, sine), (dk, decay), (cw, conv_w), (cb, conv_b), (lg, ln_g), (lb, ln_b)):
                sp.dma_start(dst, src).then_inc(tables_in, 16)
            sp.dma_start(g2, ffn_g.partition_broadcast(P)).then_inc(gains_in, 16)
            for c in range(1, len(chunks)):
                if chunks[c] == ("out", 0):
                    wait_unit(sp, "xT", NT, 1)
                    sp.dma_start(X, x.rearrange("(t p) d -> p t d", p=P)).then_inc(x_again, 16)
                if chunks[c][0] == "q":
                    for hp in range(4 * chunks[c][1], 4 * chunks[c][1] + 4):
                        if hp >= 2:
                            wait_unit(sp, "s", hp - 2)
                        if hp == 4 * chunks[c][1] + 0:
                            load_chunk(c)
                        sp.dma_start(key_t[:, hp % 2, :], keys[:, hp, :]).then_inc(key_in[hp % 2], 16)
                else:
                    load_chunk(c)
            sp.wait_ge(w_ready, GROUPS)
            sp.dma_start(x_cur, final_g.partition_broadcast(P)).then_inc(g_final_in, 16)
            for t in range(NT):
                sp.wait_ge(y_out, t + 1)
                sp.dma_start(out[t * P:(t + 1) * P, :], xn2[:, t, :]).then_inc(stored, 16)
            sp.wait_ge(stored, 16 * NT)

        @block.tensor
        def _(pe):
            def open_bank(stage, i, j=0):
                u = at[stage, i, j]
                if u >= BANKS:
                    owner, n = nth[u - BANKS]
                    pe.wait_ge(emptied[owner], n)
                return banks[u % BANKS]

            def product(out_ap, pairs):
                for n, (lhs, rhs) in enumerate(pairs):
                    last = nc.tensor.matmul(out_ap, lhs, rhs, start=n == 0, stop=n == len(pairs) - 1)
                return last

            def transpose_tile(stage, t, src):
                for half in range(2):
                    bank = open_bank(stage, t, half)
                    for i in range(4):
                        k = 4 * half + i
                        last = nc.tensor.transpose(bank[:, i * P:(i + 1) * P], src[:, k * P:(k + 1) * P], ident)
                    last.then_inc(unit_done, 1)

            def channels_first(stage, n, cuts):
                w = wait_chunk(pe, "in", n)
                for m in range(4):
                    for j, (a, b) in enumerate(cuts):
                        bank = open_bank(stage, m, j)
                        product(bank[:, 0:b - a], [(w[:, k, m * P:(m + 1) * P], xT[:, k, a:b]) for k in range(KD)]).then_inc(unit_done, 1)

            def tokens_first(stage, i, name, n, lhs_of, tiles, cut=None):
                w = wait_chunk(pe, name, n)
                for t in tiles:
                    bank = open_bank(stage, i, t)
                    lhs = lhs_of(t)
                    kd = len(lhs)
                    cols = slice(0, N) if cut is None else cut
                    product(bank[0:lhs[0].shape[1], :], [(lhs[k], w[:, k, cols]) for k in range(kd)]).then_inc(unit_done, 1)

            def x_tile(t):
                a = META + t * P
                return [xT[:, k, a:a + P] for k in range(KD)]

            pe.wait_ge(ident_in, 16)
            pe.wait_ge(normed, 1)
            bank = open_bank("xT", 0)
            for k in range(KD):
                last = nc.tensor.transpose(bank[:, k * META:(k + 1) * META], meta_t[0:META, k * P:(k + 1) * P], ident[0:META, 0:META])
            last.then_inc(unit_done, 1)
            for t in range(NT):
                pe.wait_ge(normed, t + 2)
                transpose_tile("xT", t + 1, X[:, t, :])
            wait_emptied(pe, "xT", NT, 1)

            channels_first("b", 1, spans)
            channels_first("a", 0, spans)
            channels_first("q", 2, [(META, L)])
            channels_first("k", 3, spans)
            for n in range(2):
                tokens_first("v", n, "in", 4 + n, lambda t: x_tile(t - 1) if t else [xT[:, k, 0:META] for k in range(KD)], range(NT + 1))
            for n in range(2):
                tokens_first("g", n, "in", 6 + n, x_tile, range(NT))

            key_tiles = [(0, META)] + [(META + t * P, P) for t in range(NT)]
            wait_emptied(pe, "v", 1, NT)
            for h in range(HEADS + 1):
                if h < HEADS:
                    wait_emptied(pe, "k", h, 1)
                    for j, (a, rows) in enumerate(key_tiles):
                        first = 0 if j == 0 else (j - 1) * P
                        bank = open_bank("sc", h, j)
                        nc.tensor.matmul(bank[0:rows, 0:T - first], k_t[:, h, a:a + rows], q_t[:, h, first:T], start=True, stop=True).then_inc(unit_done, 1)
                if h > 0:
                    g = h - 1
                    pe.wait_ge(p_ready, (NT + 1) * h)
                    for i in range(NT):
                        bank = open_bank("pv", g, i)
                        pairs = [(p_buf[0:META, g % 2, i * P:(i + 1) * P], v_meta[0:META, g * DV:(g + 1) * DV])]
                        for j in range(i + 1):
                            a = p_at[j + 1] + (i - j) * P
                            pairs.append((p_buf[:, g % 2, a:a + P], v_x[:, j, g * DV:(g + 1) * DV]))
                        product(bank[:, 0:DV], pairs).then_inc(unit_done, 1)

            tokens_first("gc", 0, "in", 8, x_tile, range(NT))
            pe.wait_ge(conv_done, CT)
            bank = open_bank("mean", 0)
            product(bank, [(ones, cv[:, c, :]) for c in range(CT)]).then_inc(unit_done, 1)
            tokens_first("gc", 1, "in", 9, x_tile, range(NT))
            tokens_first("gr", 0, "in", 10, x_tile, range(NT))
            pe.wait_ge(squared, CT)
            bank = open_bank("var", 0)
            product(bank, [(ones, squares[:, c, :]) for c in range(CT)]).then_inc(unit_done, 1)
            tokens_first("gr", 1, "in", 11, x_tile, range(NT))

            pe.wait_ge(og_done, HEADS * NT)
            for t in range(NT):
                transpose_tile("oT", t, big_a[:, t, :])
            pe.wait_ge(conv_act, CT)
            for n in range(2):
                tokens_first("cp", n, "conv", 0, lambda t: [cv[:, c, t * P:(t + 1) * P] for c in range(CT)], range(NT), slice(n * N, (n + 1) * N))
            wait_emptied(pe, "oT", NT - 1, 1)
            for n in range(2):
                tokens_first("rp", n, "ret", n, lambda t: [oT[:, k, t * P:(t + 1) * P] for k in range(KD)], range(NT))
            for t in range(NT):
                pe.wait_ge(merged, NT + t + 1)
                transpose_tile("mT", t, big_b[:, t, :])
            wait_emptied(pe, "mT", NT - 1, 1)
            for n in range(2):
                tokens_first("wo", n, "out", n, lambda t: [mT[:, k, t * P:(t + 1) * P] for k in range(KD)], range(NT))

            for t in range(NT):
                pe.wait_ge(xn2_ready, t + 1)
                transpose_tile("zT", t, xn2[:, t, :])
            wait_emptied(pe, "zT", NT - 1, 1)
            for hp in range(2 * PH + 1):
                if hp < 2 * PH:
                    w = wait_chunk(pe, "q", hp // 4)
                    m = hp % 4
                    bank = open_bank("wq", hp)
                    product(bank, [(w[:, k, m * P:(m + 1) * P], oT[:, k, :]) for k in range(KD)]).then_inc(unit_done, 1)
                if hp > 0:
                    g = hp - 1
                    wait_emptied(pe, "wq", g)
                    pe.wait_ge(key_in[g % 2], 16 * (g // 2 + 1))
                    bank = open_bank("s", g)
                    for t in range(NT):
                        last = nc.tensor.matmul(bank[:, t * NK:(t + 1) * NK], q_top[:, g % 2, t * P:(t + 1) * P], key_t[:, g % 2, :], start=True, stop=True)
                    last.then_inc(unit_done, 1)

            y = [banks[0], banks[1]]
            wait_emptied(pe, "s", 2 * PH - 1)
            with pe.Fori(0, NT) as t:
                pe.wait_ge(y_copied, t * 2 + 1)
                for n in range(2):
                    nc.tensor.matmul(y[n], ident, X_flat[:, bass.ds(t * D + n * N, N)], start=True, stop=False)
                with pe.Fori(0, PH // 2) as half:
                    group = t * PH + half * 2
                    for k in range(2 * TOP):
                        pe.wait_ge(diag_ready, group * TOP + (k + 1))
                        pe.wait_ge(v_in[k % SLOTS], group * (16 * TOP // SLOTS) + 16 * (k // SLOTS + 1))
                        for n in range(2):
                            last = nc.tensor.matmul(y[n], diag[:, k % SLOTS, :], v_ring[:, k % SLOTS, n * N:(n + 1) * N], start=False, stop=False)
                        last.then_inc(v_used, 1)
                for n in range(2):
                    last = nc.tensor.matmul(y[n][:, 0:2], zeros, zeros[:, 0:2], start=False, stop=True)
                last.then_inc(y_done, 1)

        @block.scalar
        def _(act):
            A = nc.scalar.activation
            act.wait_ge(x_in, 32)
            roots = [0]

            def rms(src, junk, at, count, ready, rows=P):
                roots[0] += 1
                column = stat[0:rows, at:at + 1]
                A(junk, src, ACT.Square, accum_out=column).then_inc(act_step, 1)
                act.wait_ge(act_step, roots[0])
                A(column, column, ACT.Sqrt, scale=1.0 / count, bias=eps[0:rows, :]).then_inc(ready, 1)

            act.wait_ge(consts_set, 1)
            rms(meta_t[0:META, :], tmp_wide[0:META, :], 0, D, ssq_ready, META)
            for t in range(NT):
                rms(X[:, t, :], tmp_wide, t + 1, D, ssq_ready)

            def empty(stage, i, j, dst, shape=None, func=ACT.Copy):
                bank = wait_unit(act, stage, i, j)
                src = bank[0:dst.shape[0], :] if shape is None else shape(bank)
                A(dst, src, func).then_inc(emptied["act"], 1)

            empty("xT", 0, 0, xT[:, :, 0:META], lambda b: b[:, 0:KD * META].rearrange("p (k t) -> p k t", k=KD))
            four = lambda b: b[:, :].rearrange("p (k t) -> p k t", k=4)
            for t in range(NT):
                for i in range(2):
                    empty("xT", t + 1, i, xT[:, 4 * i:4 * i + 4, META + t * P:META + (t + 1) * P], four)
            for c in range(CT):
                for i, (a, b) in enumerate(spans):
                    empty("b", c, i, sig_b[:, c, a:b], lambda bank: bank[:, 0:HALF], ACT.Sigmoid)
            swaps = [("q", h, 0, T) for h in range(HEADS)] + [("k", h, i, HALF) for h in range(HEADS) for i in range(2)]
            for n, (stage, h, i, width) in enumerate(swaps):
                bank = wait_unit(act, stage, h, i)
                if n >= 2:
                    act.wait_ge(swap_used, n - 1)
                A(tmp[0:64, n % 2, 0:width], bank[64:128, 0:width], ACT.Copy).then_inc(swapped, 1)
                A(tmp[64:128, n % 2, 0:width], bank[0:64, 0:width], ACT.Copy).then_inc(swapped, 1)
            for n in range(2):
                for t in range(NT + 1):
                    dst = v_x[:, t - 1, n * N:(n + 1) * N] if t else v_meta[0:META, n * N:(n + 1) * N]
                    empty("v", n, t, dst)
            for n in range(2):
                for t in range(NT):
                    bank = wait_unit(act, "g", n, t)
                    u = n * NT + t
                    if u >= 2:
                        act.wait_ge(gsig_used, u - 1)
                    A(tmp[:, 2 + u % 2, :], bank, ACT.Sigmoid).then_inc(gsig_ready, 1)
            for h in range(HEADS):
                for i in range(NT):
                    bank = wait_unit(act, "pv", h, i)
                    u = h * NT + i
                    rms(bank[:, 0:DV], tmp[:, 0, 0:DV], 8 + u, DV, pv_ssq)
            for t in range(NT):
                empty("gc", 0, t, big_b[:, t, 0:N], None, ACT.Sigmoid)
            for c in range(CT):
                act.wait_ge(centered, c + 1)
                A(squares[:, c, :], cv[:, c, :], ACT.Square).then_inc(squared, 1)
            for t in range(NT):
                empty("gc", 1, t, big_b[:, t, N:D], None, ACT.Sigmoid)
            for t in range(NT):
                empty("gr", 0, t, big_c[:, t, 0:N], None, ACT.Sigmoid)
            wait_emptied(act, "var", 0)
            A(tmp[:, 0, :], tmp[:, 0, :], ACT.Sqrt).then_inc(root_ready, 1)
            for c in range(CT):
                act.wait_ge(scaled, c + 1)
                A(squares[:, c, :], cv[:, c, :], ACT.Sigmoid, scale=lg[:, c:c + 1], bias=lb[:, c:c + 1]).then_inc(conv_sig, 1)
            for t in range(NT):
                empty("gr", 1, t, big_c[:, t, N:D], None, ACT.Sigmoid)
            for t in range(NT):
                for i in range(2):
                    empty("oT", t, i, oT[:, 4 * i:4 * i + 4, t * P:(t + 1) * P], four)
            for t in range(NT):
                for i in range(2):
                    empty("mT", t, i, mT[:, 4 * i:4 * i + 4, t * P:(t + 1) * P], four)
            for t in range(NT):
                act.wait_ge(h_ready, NT + t + 1)
                rms(X[:, t, :], tmp_wide, 24 + t, D, h_ssq)
            for t in range(NT):
                for i in range(2):
                    empty("zT", t, i, oT[:, 4 * i:4 * i + 4, t * P:(t + 1) * P], four)
            for hp in range(2 * PH + 1):
                if hp < 2 * PH:
                    if hp >= 2:
                        wait_unit(act, "s", hp - 2)
                    empty("wq", hp, 0, q_top[:, hp % 2, :])
                if hp > 0:
                    empty("s", hp - 1, 0, scores_t[:, :, hp - 1, :], four)
                    wait_emptied(act, "s", hp - 1)
                    act.sem_inc(scores_ready, 3 if hp == 2 * PH else 1)

            def softmax(count):
                act.wait_ge(top_ready, count)
                A(gate_exp, small["top"], ACT.Exp, bias=soft[:, 0:1], accum_out=soft[:, 1:2]).then_inc(soft_ready, 1)

            softmax(1)
            with act.Fori(0, NT) as t:
                with act.Fori(0, PH // 2) as half:
                    for i in range(2):
                        group = t * PH + half * 2 + i
                        act.wait_ge(arg_ready, group + 1)
                        A(small["th"], small["arg"], ACT.Tanh, scale=float(np.sqrt(2 / np.pi))).then_inc(tanh_ready, 1)
                        act.wait_ge(w_ready, group + 1)
                        for k in range(TOP):
                            act.wait_ge(v_used, group * TOP + (k + 1))
                            A(diag[:, k % SLOTS, :], ident, ACT.Copy, scale=weights[:, i * TOP + k:i * TOP + k + 1]).then_inc(diag_ready, 1)
                        softmax(group + 2)
                act.wait_ge(y_done, t + 1)
                for n in range(2):
                    A(X_flat[:, bass.ds(t * D + n * N, N)], banks[n], ACT.Copy).then_inc(y_copied, 1)
            act.wait_ge(y_copied, 2 * NT + 1)
            for t in range(NT):
                rms(X[:, t, :], final_sq, 40 + t, D, fin_ssq)

        @block.vector
        def _(dve):
            TT, TS, STT = nc.vector.tensor_tensor, nc.vector.tensor_scalar, nc.vector.scalar_tensor_tensor
            steps = [0]

            def link(ins):
                steps[0] += 1
                ins.then_inc(dve_step, 1)
                dve.wait_ge(dve_step, steps[0])

            nc.vector.memset(zeros, 0.0)
            nc.vector.memset(eps, EPS)
            nc.vector.memset(ones, 1.0 / CONV)
            nc.vector.memset(hb[:, :, 0:PAD], 0.0).then_inc(consts_set, 1)
            dve.wait_ge(consts_set, 1)

            dve.wait_ge(gains_in, 32)
            dve.wait_ge(ssq_ready, 1)
            link(nc.vector.reciprocal(stat[0:META, 0:1], stat[0:META, 0:1]))
            STT(meta_t[0:META, :], meta_t[0:META, :], stat[0:META, 0:1], g1[0:META, :], ALU.mult, ALU.mult).then_inc(normed, 1)
            for t in range(NT):
                dve.wait_ge(ssq_ready, t + 2)
                link(nc.vector.reciprocal(stat[:, t + 1:t + 2], stat[:, t + 1:t + 2]))
                STT(X[:, t, :], X[:, t, :], stat[:, t + 1:t + 2], g1, ALU.mult, ALU.mult).then_inc(normed, 1)

            dve.wait_ge(tables_in, 16 * 7)
            for c in range(CT):
                for i, (a, b) in enumerate(spans):
                    wait_emptied(dve, "b", c, i)
                    bank = wait_unit(dve, "a", c, i)
                    TT(hb[:, c, PAD + a:PAD + b], bank[:, 0:HALF], sig_b[:, c, a:b], ALU.mult).then_inc(emptied["dve"], 1)

            def rotate(n, stage, h, i, dst, a, b):
                bank = wait_unit(dve, stage, h, i)
                dve.wait_ge(swapped, 2 * (n + 1))
                link(TT(dst, bank[:, 0:b - a], cosv[:, a:b], ALU.mult))
                link(TT(tmp[:, n % 2, 0:b - a], tmp[:, n % 2, 0:b - a], sinv[:, a:b], ALU.mult))
                TT(dst, dst, tmp[:, n % 2, 0:b - a], ALU.add).then_inc(emptied["dve"], 1)
                wait_emptied(dve, stage, h, i)
                dve.sem_inc(swap_used, 1)

            def convolve(c):
                link(TS(cv[:, c, :], hb[:, c, 0:T], cw[:, c, 0:1], cb[:, c:c + 1], ALU.mult, ALU.add))
                for w in range(1, TAPS):
                    ins = STT(cv[:, c, :], hb[:, c, w:w + T], cw[:, c, w:w + 1], cv[:, c, :], ALU.mult, ALU.add)
                    if w < TAPS - 1:
                        link(ins)
                ins.then_inc(conv_done, 1)

            for h in range(HEADS):
                rotate(h, "q", h, 0, q_t[:, h, :], META, L)
            wait_emptied(dve, "a", CT - 1, 1)
            convolve(0)
            n = HEADS
            for h in range(HEADS):
                for i, (a, b) in enumerate(spans):
                    rotate(n, "k", h, i, k_t[:, h, a:b], a, b)
                    n += 1
            convolve(1)
            for n in range(2):
                for t in range(NT):
                    u = n * NT + t
                    bank = wait_unit(dve, "g", n, t)
                    dve.wait_ge(gsig_ready, u + 1)
                    TT(big_a[:, t, n * N:(n + 1) * N], bank, tmp[:, 2 + u % 2, :], ALU.mult).then_inc(emptied["dve"], 1)
                    wait_emptied(dve, "g", n, t)
                    dve.sem_inc(gsig_used, 1)
                convolve(2 + n)

            for h in range(HEADS + 1):
                if h < HEADS:
                    if h >= 2:
                        wait_unit(dve, "pv", h - 2, NT - 1)
                    for j in range(NT + 1):
                        bank = wait_unit(dve, "sc", h, j)
                        rows, first, d0 = (META, 0, META) if j == 0 else (P, (j - 1) * P, 0)
                        a = p_at[j]
                        TT(p_buf[0:rows, h % 2, a:a + T - first], bank[0:rows, 0:T - first], dk[0:rows, h, d0:d0 + T - first], ALU.mult).then_inc(emptied["dve"], 1)
                        wait_emptied(dve, "sc", h, j)
                        dve.sem_inc(p_ready, 1)
                if h > 0:
                    g = h - 1
                    for i in range(NT):
                        u = g * NT + i
                        bank = wait_unit(dve, "pv", g, i)
                        dve.wait_ge(pv_ssq, u + 1)
                        link(nc.vector.reciprocal(stat[:, 8 + u:9 + u], stat[:, 8 + u:9 + u]))
                        cols = big_a[:, i, g * DV:(g + 1) * DV]
                        STT(cols, bank[:, 0:DV], stat[:, 8 + u:9 + u], cols, ALU.mult, ALU.mult).then_inc(emptied["dve"], 1)
                        wait_emptied(dve, "pv", g, i)
                        dve.sem_inc(og_done, 1)

            bank = wait_unit(dve, "mean", 0)
            dve.wait_ge(conv_done, CT)
            for c in range(CT):
                ins = TT(cv[:, c, :], cv[:, c, :], bank, ALU.subtract)
                ins.then_inc(centered, 1)
            dve.wait_ge(centered, CT)
            dve.sem_inc(emptied["dve"], 1)
            bank = wait_unit(dve, "var", 0)
            TS(tmp[:, 0, :], bank, EPS, None, ALU.add).then_inc(emptied["dve"], 1)
            dve.wait_ge(root_ready, 1)
            link(nc.vector.reciprocal(tmp[:, 1, :], tmp[:, 0, :]))
            for c in range(CT):
                dve.wait_ge(squared, c + 1)
                TT(cv[:, c, :], cv[:, c, :], tmp[:, 1, :], ALU.mult).then_inc(scaled, 1)
            for c in range(CT):
                dve.wait_ge(conv_sig, c + 1)
                link(TS(cv[:, c, :], cv[:, c, :], lg[:, c:c + 1], lb[:, c:c + 1], ALU.mult, ALU.add))
                TT(cv[:, c, :], cv[:, c, :], squares[:, c, :], ALU.mult).then_inc(conv_act, 1)

            for n in range(2):
                for t in range(NT):
                    wait_emptied(dve, "gc", n, t)
                    bank = wait_unit(dve, "cp", n, t)
                    cols = big_b[:, t, n * N:(n + 1) * N]
                    TT(cols, bank, cols, ALU.mult).then_inc(emptied["dve"], 1)
            for n in range(2):
                for t in range(NT):
                    wait_emptied(dve, "gr", n, t)
                    wait_emptied(dve, "cp", n, t)
                    bank = wait_unit(dve, "rp", n, t)
                    cols, gated = big_b[:, t, n * N:(n + 1) * N], big_c[:, t, n * N:(n + 1) * N]
                    TT(gated, bank, gated, ALU.mult).then_inc(emptied["dve"], 1)
                    wait_emptied(dve, "rp", n, t)
                    TT(cols, cols, gated, ALU.add).then_inc(merged, 1)

            dve.wait_ge(x_again, 16)
            for n in range(2):
                for t in range(NT):
                    bank = wait_unit(dve, "wo", n, t)
                    cols = X[:, t, n * N:(n + 1) * N]
                    TT(cols, bank, cols, ALU.add).then_inc(emptied["dve"], 1)
                    wait_emptied(dve, "wo", n, t)
                    dve.sem_inc(h_ready, 1)
            for t in range(NT):
                dve.wait_ge(h_ssq, t + 1)
                link(nc.vector.reciprocal(stat[:, 24 + t:25 + t], stat[:, 24 + t:25 + t]))
                STT(xn2[:, t, :], X[:, t, :], stat[:, 24 + t:25 + t], g2, ALU.mult, ALU.mult).then_inc(xn2_ready, 1)

            def route(parity, before_idx):
                pair, rest, vals, keyf = small["pair"], small["rest"], small["vals"], small["keyf"]
                for side in range(2):
                    src = pair[:, side * NK:(side + 1) * NK]
                    v8 = [vals[:, side * TOP + 8 * i:side * TOP + 8 * i + 8] for i in range(2)]
                    i8 = [ids[:, side * TOP + 8 * i:side * TOP + 8 * i + 8] for i in range(2)]
                    chain(nc.vector.max(v8[0], src))
                    chain(nc.vector.max_index(i8[0], v8[0], src))
                    chain(nc.vector.match_replace(rest, v8[0], src, LOWEST))
                    chain(nc.vector.max(v8[1], rest))
                    chain(nc.vector.max_index(i8[1], v8[1], rest))
                chain(nc.vector.tensor_copy(keyf, ids))
                grid = pair_scores.rearrange("p (i j) -> p i j", i=TOP)
                chain(TT(grid, vals[:, 0:TOP].unsqueeze(2).broadcast_to([P, TOP, TOP]),
                         vals[:, TOP:2 * TOP].unsqueeze(1).broadcast_to([P, TOP, TOP]), ALU.add))
                top = small["top"]
                chain(nc.vector.max(top[:, 0:8], pair_scores))
                chain(nc.vector.max_index(pos[:, 0:8], top[:, 0:8], pair_scores))
                chain(nc.vector.match_replace(rest2, top[:, 0:8], pair_scores, LOWEST))
                chain(nc.vector.max(top[:, 8:16], rest2))
                chain(TS(soft[:, 0:1], top[:, 0:1], -1.0, None, ALU.mult))
                dve.sem_inc(top_ready, 1)
                chain(nc.vector.max_index(pos[:, 8:16], top[:, 8:16], rest2))
                chain(TS(pos[:, TOP:2 * TOP], pos[:, 0:TOP], 4, None, ALU.logical_shift_right))
                chain(TS(pos[:, 2 * TOP:3 * TOP], pos[:, 0:TOP], TOP - 1, None, ALU.bitwise_and))
                chain(nc.vector.tensor_copy(small["posf"], pos[:, TOP:3 * TOP]))
                hot3 = hot.rearrange("p (k j) -> p k j", k=TOP)
                for side in range(2):
                    place = small["posf"][:, side * TOP:(side + 1) * TOP].unsqueeze(2).broadcast_to([P, TOP, TOP])
                    chain(TT(hot3, place, small["iota"].unsqueeze(1).broadcast_to([P, TOP, TOP]), ALU.is_equal))
                    chain(TT(hot3, hot3, keyf[:, side * TOP:(side + 1) * TOP].unsqueeze(1).broadcast_to([P, TOP, TOP]), ALU.mult))
                    chain(nc.vector.tensor_reduce(small["chosen"][:, side * TOP:(side + 1) * TOP], hot3, AX.X, ALU.add))
                before_idx()
                chain(STT(experts[:, parity * TOP:(parity + 1) * TOP], small["chosen"][:, 0:TOP], float(NK), small["chosen"][:, TOP:2 * TOP], ALU.mult, ALU.add))
                dve.sem_inc(idx_ready, 1)

            chained = [0]

            def chain(ins):
                chained[0] += 1
                ins.then_inc(group_step, 1)
                dve.wait_ge(group_step, chained[0])

            link(nc.vector.memset(scores[:, GROUPS * 2 * NK:(GROUPS + 1) * 2 * NK], 0.0))
            nc.vector.memset(small["gate"], 0.0).then_inc(u_used, SLOTS)
            dve.sem_inc(v_used, SLOTS)
            dve.sem_inc(y_copied, 1)
            dve.wait_ge(u_used, SLOTS)
            dve.wait_ge(iota_set, 1)
            dve.wait_ge(scores_ready, 2)
            chain(nc.vector.tensor_copy(small["pair"], scores[:, 0:2 * NK]))
            route(0, lambda: None)
            with dve.Fori(0, NT) as t:
                nc.vector.tensor_copy(x_cur, xn2_flat[:, bass.ds(t * D, D)]).then_inc(tile_set, 1)
                with dve.Fori(0, PH // 2) as half:
                    for i in range(2):
                        group = t * PH + half * 2 + i
                        dve.sem_clear(group_step)
                        chained[0] = 0
                        dve.wait_ge(tile_set, t + 1)
                        for k in range(TOP):
                            dve.wait_ge(u_in[k % SLOTS], group * (16 * TOP // SLOTS) + 16 * (k // SLOTS + 1))
                            nc.vector.tensor_tensor_reduce(out=junk, in0=u_ring[:, k % SLOTS, :], in1=x_cur, scale=1.0, scalar=0.0,
                                                           op0=ALU.mult, op1=ALU.add, accum_out=small["act"][:, k:k + 1]).then_inc(u_used, 1)
                            dve.wait_ge(u_used, group * TOP + (SLOTS + k + 1))
                        dots, arg = small["act"], small["arg"]
                        chain(TT(arg, dots, dots, ALU.mult))
                        chain(TS(arg, arg, 0.044715, 1.0, ALU.mult, ALU.add))
                        chain(TT(arg, arg, dots, ALU.mult))
                        dve.sem_inc(arg_ready, 1)
                        dve.wait_ge(tanh_ready, group + 1)
                        chain(STT(arg, small["th"], 1.0, dots, ALU.add, ALU.mult))
                        dve.wait_ge(soft_ready, group + 1)
                        chain(nc.vector.reciprocal(soft[:, 2:3], soft[:, 1:2]))
                        chain(TS(small["gate"], gate_exp, soft[:, 2:3], 0.5, ALU.mult, ALU.mult))
                        chain(TT(weights[:, i * TOP:(i + 1) * TOP], arg, small["gate"], ALU.mult))
                        dve.sem_inc(w_ready, 1)
                        dve.wait_ge(scores_ready, half * 4 + (2 * i + 4))
                        chain(nc.vector.tensor_copy(small["pair"], scores[:, bass.ds(group * 2 * NK + 2 * NK, 2 * NK)]))
                        route(1 - i, lambda: dve.wait_ge(v_used, group * TOP + SLOTS))

            dve.wait_ge(g_final_in, 16)
            for t in range(NT):
                dve.wait_ge(fin_ssq, t + 1)
                link(nc.vector.reciprocal(stat[:, 40 + t:41 + t], stat[:, 40 + t:41 + t]))
                STT(xn2[:, t, :], X[:, t, :], stat[:, 40 + t:41 + t], x_cur, ALU.mult, ALU.mult).then_inc(y_out, 1)

        @block.gpsimd
        def _(pool):
            wait_emptied(pool, "g", 1, NT - 1)
            nc.gpsimd.iota(small["iota"], pattern=[[1, TOP]], base=0, channel_multiplier=0, allow_small_or_imprecise_dtypes=True).then_inc(iota_set, 1)
            wait_unit(pool, "mT", NT - 1, 1)
            with pool.Fori(0, GROUPS, 2) as group:
                for i in range(2):
                    pool.wait_ge(idx_ready, group + (i + 1))
                    for table, ring, arrived, used in ((peer_u, u_ring, u_in, u_used), (peer_v, v_ring, v_in, v_used)):
                        for k in range(TOP):
                            pool.wait_ge(used, group * TOP + (i * TOP + k + 1))
                            pool.sem_inc(slots_found, 1)
                            pool.indirect_dma_start(ring[:, k % SLOTS, :], None, table,
                                                    bass.IndirectOffsetOnAxis(experts[:, i * TOP + k:i * TOP + k + 1], 0)).then_inc(arrived[k % SLOTS], 16)


_NAMES = ["x", "meta", "w_in", "conv_w", "conv_b", "ln_g", "ln_b", "conv_proj", "ret_proj", "w_out", "mix_g", "ffn_g",
          "final_g", "peer_wq", "keys", "peer_u", "peer_v", "cosine", "sine", "decay", "identity"]


def _tables():
    half = P // 2
    freqs = np.float32(10000.0) ** (-np.arange(half, dtype=np.float32) / np.float32(half))
    angle = np.arange(L, dtype=np.float32)[None, :] * freqs[:, None]
    cosine = np.concatenate([np.cos(angle)] * 2).astype(np.float32)
    sine = np.concatenate([-np.sin(angle), np.sin(angle)]).astype(np.float32)
    log_gamma = np.log(1.0 - 2.0 ** (-5.0 - np.arange(HEADS)))
    distance = np.arange(L)[None, None, :] - np.arange(P)[:, None, None]
    decay = np.where(distance >= 0, np.exp(log_gamma[None, :, None] * np.maximum(distance, 0)), 0.0) * P ** -0.5
    return {"cosine": cosine, "sine": sine, "decay": decay.astype(np.float32), "identity": np.eye(P, dtype=np.float32)}


def kernel(x, meta_tokens, norm_mix_g, w_in, conv_dw_w, conv_dw_b, conv_ln_g, conv_ln_b, conv_proj_w, ret_proj_w,
           w_out, norm_ffn_g, peer_w_q, peer_sub_keys, peer_u, peer_v, norm_final_g):
    import concourse.bacc as bacc
    from concourse.bass_utils import run_bass_kernel_spmd

    def channels(a):
        return np.moveaxis(np.asarray(a).reshape(-1, CT, P), (2, 1), (0, 1))

    given = {
        "x": np.asarray(x)[0], "meta": np.asarray(meta_tokens), "w_in": np.asarray(w_in)[0],
        "conv_w": channels(np.asarray(conv_dw_w)[0]),
        "conv_b": channels(conv_dw_b[0])[:, :, 0], "ln_g": channels(conv_ln_g[0])[:, :, 0], "ln_b": channels(conv_ln_b[0])[:, :, 0],
        "conv_proj": np.asarray(conv_proj_w)[0], "ret_proj": np.asarray(ret_proj_w)[0], "w_out": np.asarray(w_out)[0],
        "mix_g": np.asarray(norm_mix_g)[0], "ffn_g": np.asarray(norm_ffn_g)[0], "final_g": np.asarray(norm_final_g),
        "peer_wq": np.asarray(peer_w_q)[0],
        "keys": np.transpose(np.asarray(peer_sub_keys)[0].reshape(2 * PH, NK, P), (2, 0, 1)),
        "peer_u": np.asarray(peer_u)[0], "peer_v": np.asarray(peer_v)[0], **_tables(),
    }
    nc = bacc.Bacc("TRN2", target_bir_lowering=False, num_devices=1)
    arrays, args = {}, []
    for name in _NAMES:
        arrays[f"in_{name}"] = np.ascontiguousarray(given[name])
        args.append(nc.dram_tensor(f"in_{name}", arrays[f"in_{name}"].shape, f32, kind="ExternalInput").ap())
    out = nc.dram_tensor("out_y", (T, D), f32, kind="ExternalOutput").ap()
    block_kernel(nc, *args, out)
    result = run_bass_kernel_spmd(nc, [arrays], core_ids=[0])
    return result.results[0]["out_y"].reshape(1, T, D)
```

```python
from contextlib import ExitStack

import numpy as np

import concourse.bass as bass
from concourse import mybir

P = 128
D = 1024
T = 512
META = 16
L = META + T
NT = T // P
KD = D // P
CONV = 512
TAPS = 31
CT = CONV // P
HEADS = 4
DV = 256
PAD = TAPS - 1 - META
N = 512
HALF = L // 2
PH = 8
NK = 128
TOP = 16
GROUPS = NT * PH
SLOTS = 8
BANKS = 8
FIRST_BESIDE = 8
EPS = 1e-6
AHEAD = 30
HEADS_FROM = 102
LOWEST = -3.4e38

f32 = mybir.dt.float32
f32r = mybir.dt.float32r
bf16 = mybir.dt.bfloat16
u32 = mybir.dt.uint32
ALU = mybir.AluOpType
ACT = mybir.ActivationFunctionType
AX = mybir.AxisListType


REST = range(1, NT)


def first_units():
    units = [("xT", 0, 0, "act")] + [("xT", t, i, "dve") for t in range(1, NT + 1) for i in range(2)]
    units += [("b", c, i, "act") for c in range(CT) for i in range(2)]
    units += [("a", c, i, "dve") for c in range(CT) for i in range(2)]
    units += [("q", h, 0, "dve") for h in range(HEADS)]
    units += [("k", h, i, "dve") for h in range(HEADS) for i in range(2)]
    units += [("v", n, t, "act") for n in range(2) for t in range(NT + 1)]
    units += [("g", n, t, "dve") for n in range(2) for t in range(NT)]
    for h in range(HEADS + 1):
        if h < HEADS:
            units += [("sc", h, j, "dve") for j in range(NT + 1)]
        if h > 0:
            units += [("pv", h - 1, i, "dve") for i in range(NT)]
    units += [("gr", 0, 0, "act")]
    units += [("gc", 0, t, "act") for t in range(NT)]
    units += [("mean", 0, 0, "dve")]
    units += [("gc", 1, t, "act") for t in range(NT)]
    units += [("var", 0, 0, "dve")]
    units += [("gr", 1, 0, "act")]
    units += [("oT", 0, i, "act") for i in range(2)]
    units += [(stage, n, 0, "dve") for stage in ("rp", "cp") for n in range(2)]
    units += [("mT", 0, i, "act") for i in range(2)]
    units += [("wo", n, 0, "dve") for n in range(2)]
    units += [("oT", t, i, "dve") for t in REST for i in range(2)]
    units += [("zT", 0, i, "act") for i in range(2)]
    for h in range(PH + 1):
        if h < PH:
            units += [("wq0", h, 0, "act")]
        if h > 0:
            units += [("s0", h - 1, 0, "act")]
    return units


def background():
    units = [("cp", n, t, "dve", 4) for t in REST for n in range(2)]
    for n in range(2):
        units += [("gr", n, t, "act", 8) for t in REST]
        units += [("rp", n, t, "dve", 8) for t in REST]
    units += [("mT", t, i, "act", 0.35) for t in REST for i in range(2)]
    units += [("wo", n, t, "dve", 8) for t in REST for n in range(2)]
    units += [("zT", t, i, "act", 0.35) for t in REST for i in range(2)]
    for hp in range(2 * PH + 1):
        if hp < 2 * PH:
            units += [("wq", hp, 0, "act", 6)]
        if hp > 0:
            units += [("s", hp - 1, 0, "act", 0.75)]
    head = 2 * (6 + 0.75)
    first_head = sum(u[4] for u in units if u[0] not in ("wq", "s")) + head
    at, steps = 0.0, []
    for stage, i, j, owner, weight in units:
        at += weight
        place = int(max(0.0, at - AHEAD) / (first_head - AHEAD) * HEADS_FROM)
        if at > first_head:
            place = HEADS_FROM + int((at - first_head) / head * TOP)
        place = place // TOP * TOP + FIRST_BESIDE + place % TOP * (TOP - FIRST_BESIDE) // TOP
        if at <= AHEAD:
            place = -1
        steps.append((place, "unit", stage, i, j, owner))
        if stage == "wo" and i == 1:
            steps += [(place, "act", "rms", j, 0, None), (place, "dve", "norm", j, 0, None)]
    return sorted(steps, key=lambda step: step[0])


def plan_banks():
    plan, holder, count, turn = {}, {}, {"act": 0, "dve": 0}, 0
    rest = [step[2:6] for step in background() if step[1] == "unit"]
    for n, (stage, i, j, owner) in enumerate(first_units() + rest):
        beside = n >= len(first_units())
        if beside and n == len(first_units()):
            turn = 0
        bank = 2 + turn % (BANKS - 2) if beside else turn % BANKS
        turn += 1
        count[owner] += 1
        plan[stage, i, j] = (n, bank, holder.get(bank), (owner, count[owner]))
        holder[bank] = (stage, i, j)
        if n == len(first_units()) - 1:
            plan["before the sum"] = [holder[0], holder[1]]
    return plan


def weight_chunks():
    order = [("in", n, 0) for n in (1, 0, 2, 3, 4, 5, 6, 7, 10, 8, 9, 11)]
    order += [("ret", 0, 0), ("ret", 1, 0), ("conv", 0, 0)]
    for turn in range(2):
        if turn:
            order += [("conv", 0, 1), ("in", 10, 1), ("ret", 0, 1), ("in", 11, 1), ("ret", 1, 1)]
        order += [("out", 0, turn), ("out", 1, turn)]
        order += [("q", n, turn) for n in range(4)]
    return order


def block_kernel(nc, x, meta, w_in, conv_w, conv_b, ln_g, ln_b, conv_proj, ret_proj, w_out, mix_g,
                 ffn_g, final_g, peer_wq, keys, peer_u, peer_v, cosine, sine, decay, identity, out):
    plan = plan_banks()
    steps_beside = background()
    chunks = weight_chunks()
    chunk_at = {c: n for n, c in enumerate(chunks)}
    WSLOTS = 2
    EXTRA = WSLOTS
    extra_chunks = [chunk_at["ret", 0, 0], chunk_at["out", 0, 0]]
    chunk_slot, holds = [], []
    for c in range(len(chunks)):
        chunk_slot.append(EXTRA if c in extra_chunks else sum(s != EXTRA for s in chunk_slot) % WSLOTS)
        holds.append(chunk_slot.count(chunk_slot[c]))

    ctx = ExitStack()
    with ctx:
        def sem(name):
            return ctx.enter_context(nc.semaphore(name))

        words = {}
        total = 0

        def region(name, size):
            nonlocal total
            words[name] = (total, size)
            total += size

        region("LTA", KD * L)
        region("CV", CT * T)
        region("DK", HEADS * L)
        region("SPAD", (GROUPS + 1) * 2 * NK - (KD * L + CT * T + HEADS * L))
        region("X", NT * D)
        region("KEY", 2 * 4 * NK)
        region("BIGA", NT * D)
        region("V", NT * D + D)
        region("R1", 2 * NT * D)
        HB = CT * (PAD + L)
        region("LTB", HB + KD * N // 2)
        region("W", WSLOTS * KD * N)
        region("XN2", NT * D)
        region("MT", D)
        region("G1", D)
        region("G2", D)
        region("TMP", 4 * N)
        region("IDENT", P)
        region("ONES", 2 * P)
        region("SMALL", 4 * 34 + 64)
        assert total * 4 <= 212800, total * 4
        arena = ctx.enter_context(nc.sbuf_tensor("arena", [P, total], f32))

        arena_at = nc.sbuf_base - 4 * total

        def parts(name, at, size, dtype=f32r):
            return nc.alloc_sbuf_tensor_at(name, [P, size], dtype, offset=arena_at + 4 * at)

        xhi = parts("x_high", words["LTA"][0], KD * L)[:, :].rearrange("p (k t) -> p k t", k=KD)
        xlo = parts("x_low", words["X"][0], KD * L)[:, :].rearrange("p (k t) -> p k t", k=KD)
        assert words["KEY"][0] == words["X"][0] + NT * D and words["G1"][0] == words["MT"][0] + D
        PIECE = KD * N // 2
        whi_tensors = [parts("w_high0", words["LTB"][0] + HB, PIECE), parts("w_high1", words["MT"][0], PIECE),
                       parts("w_high2", words["DK"][0], PIECE)]
        raw_tensors = [parts(f"w_whole{i}", words["W"][0] + i * KD * N, KD * N, f32) for i in range(WSLOTS)]
        meta_whole = parts("x_meta_whole", words["TMP"][0] + 3 * N, KD * META, f32)[:, :].rearrange("p (k t) -> p k t", k=KD)
        wlo_tensors = [parts(f"w_low{i}", words["W"][0] + i * KD * N, KD * N) for i in range(WSLOTS)]

        def view(name, offset=0, size=None):
            start, full = words[name]
            return arena[:, start + offset:start + offset + (full - offset if size is None else size)]

        squares = view("CV").rearrange("p (c t) -> p c t", c=CT)
        dk = view("DK").rearrange("p (h t) -> p h t", h=HEADS)
        start_s = words["LTA"][0]
        scores = arena[:, start_s:start_s + (GROUPS + 1) * 2 * NK]
        scores_t = scores[:, 0:GROUPS * 2 * NK].rearrange("p (t s k) -> p t s k", t=NT, s=2 * PH)
        rest_at = start_s + PH * 2 * NK
        rest_b = arena[:, rest_at:rest_at + 3 * D].rearrange("p (t d) -> p t d", t=3)
        x_rest = parts("x_rest", rest_at + 3 * D, 3 * D, f32)[:, :].rearrange("p (k t) -> p k t", k=KD)
        rest_gate = [view("TMP", 0, N), view("TMP", N, N), view("KEY", 0, N)]
        m_rest = arena[:, rest_at + 3 * D:rest_at + 6 * D].rearrange("p (k t) -> p k t", k=KD)
        m_first = view("V", NT * D, D).rearrange("p (k t) -> p k t", k=KD)
        X = view("X").rearrange("p (t d) -> p t d", t=NT)
        big_a = view("BIGA").rearrange("p (t d) -> p t d", t=NT)
        v_x = view("V", 0, NT * D).rearrange("p (t d) -> p t d", t=NT)
        v_meta = view("V", NT * D, D)
        q_t = view("R1", 0, HEADS * T).rearrange("p (h t) -> p h t", h=HEADS)
        k_t = view("R1", HEADS * T, HEADS * L).rearrange("p (h t) -> p h t", h=HEADS)
        TRI = T + T + 384 + 256 + 128
        p_at = [0, T, 2 * T, 2 * T + 384, 2 * T + 640]
        p_buf = view("R1", HEADS * (T + L), 2 * TRI).rearrange("p (b n) -> p b n", b=2)
        sig_b = view("R1", HEADS * (T + L), CT * L).rearrange("p (c t) -> p c t", c=CT)
        big_b = view("R1", 0, NT * D).rearrange("p (t d) -> p t d", t=NT)
        big_c = view("R1", NT * D, NT * D).rearrange("p (t d) -> p t d", t=NT)
        hb = view("LTB", 0, HB).rearrange("p (c t) -> p c t", c=CT)
        oT = view("LTB", 0, NT * D).rearrange("p (k t) -> p k t", k=KD)
        W = [view("W", i * KD * N, KD * N) for i in range(WSLOTS)] + [view("V", 0, KD * N)]
        xn2 = view("XN2").rearrange("p (t d) -> p t d", t=NT)
        cosv, sinv = view("XN2", 0, L), view("XN2", L, L)
        cv = view("XN2", 2 * L, CT * T).rearrange("p (c t) -> p c t", c=CT)
        meta_t = view("MT")
        g1, g2 = view("G1"), view("G2")
        tmp = view("TMP").rearrange("p (b n) -> p b n", b=4)
        key_t = view("KEY").rearrange("p (b s n) -> p b s n", b=2, s=4)
        ident, ones = view("IDENT"), view("ONES", 0, P)
        cw = view("SMALL", 0, CT * TAPS).rearrange("p (c w) -> p c w", c=CT)
        cb, lg, lb = (view("SMALL", CT * TAPS + i * CT, CT) for i in range(3))
        stat, eps = view("SMALL", 4 * 34, 60), view("SMALL", 4 * 34 + 60, 1)
        q_top = view("TMP", 0, 2 * N).rearrange("p (b n) -> p b n", b=2)
        ring0 = words["BIGA"][0]
        u_ring = arena[:, ring0:ring0 + SLOTS * D].rearrange("p (s d) -> p s d", s=SLOTS)
        v_ring = arena[:, ring0 + SLOTS * D:ring0 + 2 * SLOTS * D].rearrange("p (s d) -> p s d", s=SLOTS)
        diag = arena[:, ring0 + 2 * SLOTS * D:ring0 + 2 * SLOTS * D + SLOTS * P].rearrange("p (s n) -> p s n", s=SLOTS)
        x_cur = view("G1")
        junk = view("MT", 0, N).bitcast(bf16)
        small, used = {}, 0

        def little(name, size):
            nonlocal used
            small[name] = view("TMP", 2 * N + used, size)
            used += size

        for name, size in (("pair", 2 * NK), ("rest", NK), ("vals", 2 * TOP), ("keyf", 2 * TOP), ("top", TOP),
                           ("posf", 2 * TOP), ("chosen", 2 * TOP), ("act", TOP), ("arg", TOP), ("th", TOP),
                           ("gate", TOP), ("w", 2 * TOP), ("soft", 8), ("iota", TOP)):
            little(name, size)
        pair_scores = view("MT", N, TOP * TOP)
        hot = view("MT", N + TOP * TOP, TOP * TOP)
        rest2 = hot
        zeros = view("ONES", P, P)
        soft, weights = small["soft"], small["w"]
        X_flat, xn2_flat = view("X"), view("XN2")
        tmp_wide = view("TMP", 0, 2 * N)
        little("expd", TOP)
        gate_exp = small["expd"]
        little("ids", 2 * TOP)
        little("pos", 3 * TOP)
        little("experts", 2 * TOP)
        ids = small["ids"].bitcast(u32)
        pos = small["pos"].bitcast(u32)
        experts = small["experts"].bitcast(u32)
        assert used <= 2 * N, used

        banks = [ctx.enter_context(nc.psum_tensor(f"bank{i}", [P, N], f32))[:, :] for i in range(BANKS)]

        x_in = sem("x_in")
        x_tile_in = [sem(f"x_tile_in{t}") for t in range(NT)]
        tables_in = sem("tables_in")
        ident_in, g1_in, g2_in = sem("ident_in"), sem("g1_in"), sem("g2_in")
        w_in_slot = [sem(f"w_in_slot{i}") for i in range(WSLOTS + 1)]
        xhi_ready = sem("xhi_ready")
        whi_ready, wlo_ready = sem("whi_ready"), sem("wlo_ready")
        half_used = sem("half_used")
        first_piece_in = sem("first_piece_in")
        key_in = [sem(f"key_in{i}") for i in range(2)]
        unit_done = sem("unit_done")
        emptied = {"act": sem("act_emptied"), "dve": sem("dve_emptied")}
        dve_step, fin_step = sem("dve_step"), sem("fin_step")
        ssq_ready, normed = sem("ssq_ready"), sem("normed")
        consts_set = sem("consts_set")
        swapped, swap_used = sem("swapped"), sem("swap_used")
        gsig_ready, gsig_used = sem("gsig_ready"), sem("gsig_used")
        p_ready = sem("p_ready")
        pv_ssq, og_done = sem("pv_ssq"), sem("og_done")
        conv_done, centered, squared, scaled, conv_sig, conv_act = (
            sem(n) for n in ("conv_done", "centered", "squared", "scaled", "conv_sig", "conv_act"))
        merged, h_ready, h_ssq, xn2_ready = (sem(n) for n in ("merged", "h_ready", "h_ssq", "xn2_ready"))
        x_again = sem("x_again")
        scores_ready = sem("scores_ready")
        top_ready, soft_ready = sem("top_ready"), sem("soft_ready")
        idx_ready, arg_ready, tanh_ready, w_ready = (sem(n) for n in ("idx_ready", "arg_ready", "tanh_ready", "w_ready"))
        u_in = [sem(f"u_in{i}") for i in range(SLOTS)]
        v_in = [sem(f"v_in{i}") for i in range(SLOTS)]
        u_used, v_used = sem("u_used"), sem("v_used")
        diag_ready = sem("diag_ready")
        y_done, y_copied = sem("y_done"), sem("y_copied")
        slots_found, gates_moved = sem("slots_found"), sem("gates_moved")
        x_kept = sem("x_kept")
        act_step, root_ready = sem("act_step"), sem("root_ready")
        group_step, tile_set, iota_set = sem("group_step"), sem("tile_set"), sem("iota_set")
        fin_ssq, y_out, g_final_in, stored = (sem(n) for n in ("fin_ssq", "y_out", "g_final_in", "stored"))

        block = ctx.enter_context(nc.Block())

        def wait_unit(eng, stage, i, j=0):
            n, bank, _, _ = plan[stage, i, j]
            eng.wait_ge(unit_done, n + 1)
            return banks[bank]

        def wait_emptied(eng, stage, i, j=0):
            owner, n = plan[stage, i, j][3]
            eng.wait_ge(emptied[owner], n)

        def wait_chunk(eng, name, n, turn=0):
            c = chunk_at[name, n, turn]
            eng.wait_ge(w_in_slot[chunk_slot[c]], 16 * holds[c])
            return W[chunk_slot[c]].rearrange("p (k n) -> p k n", k=CT if name == "conv" else KD)

        IN_CHUNKS = 12
        PIECES = 2 * IN_CHUNKS
        BY_COLUMNS = 4

        AFTER_RETENTION = 18
        high_place = [p % 2 if p < AFTER_RETENTION else (p - AFTER_RETENTION + 2) % 3 for p in range(PIECES)]

        def piece(p):
            c, half = p // 2, p % 2
            high = whi_tensors[high_place[p]][:, :]
            places = [raw_tensors[c % WSLOTS][:, :], wlo_tensors[c % WSLOTS][:, :]]
            places = [a.rearrange("p (k n) -> p k n", k=KD) for a in places]
            if c < BY_COLUMNS:
                raw, low = (a[:, :, half * (N // 2):(half + 1) * (N // 2)] for a in places)
                return raw, high.rearrange("p (k n) -> p k n", k=KD), low
            raw, low = (a[:, half * (KD // 2):(half + 1) * (KD // 2), :] for a in places)
            return raw, high.rearrange("p (k n) -> p k n", k=KD // 2), low

        last_of = dict(zip(chunks, [("b", 3, 1), ("a", 3, 1), ("q", 3, 0), ("k", 3, 1), ("v", 0, NT), ("v", 1, NT),
                                    ("g", 0, 3), ("g", 1, 3), ("gr", 0, 0), ("gc", 0, 3), ("gc", 1, 3), ("gr", 1, 0),
                                    ("rp", 0, 0), ("rp", 1, 0), ("cp", 1, 0), ("wo", 0, 0), ("wo", 1, 0)]
                            + [("wq0", 2 * n + 1, 0) for n in range(4)]
                            + [("cp", 1, 3), ("gr", 0, 3), ("rp", 0, 3), ("gr", 1, 3), ("rp", 1, 3), ("wo", 0, 3), ("wo", 1, 3)]
                            + [("wq", 4 * n + 3, 0) for n in range(4)]))
        spans = [(0, HALF), (HALF, L)]

        @block.sync
        def _(sp):
            def first_half(half, arrived):
                cols = slice(half * (N // 2), (half + 1) * (N // 2))
                dst = raw_tensors[0][:, :].rearrange("p (k n) -> p k n", k=KD)[:, :, cols]
                src = w_in[:, chunks[0][1] * N:(chunks[0][1] + 1) * N][:, cols]
                sp.dma_start(dst, src.rearrange("(k p) n -> p k n", p=P)).then_inc(arrived, 16)

            sp.dma_start(meta_t[0:META, :], meta).then_inc(x_in, 16)
            sp.dma_start(g1, mix_g.partition_broadcast(P)).then_inc(g1_in, 16)
            sp.dma_start(ident, identity).then_inc(ident_in, 16)
            for t in range(NT):
                if t == NT - 1:
                    first_half(0, first_piece_in)
                sp.dma_start(X[:, t, :], x[t * P:(t + 1) * P, :]).then_inc(x_tile_in[t], 16)
            first_half(1, w_in_slot[0])

            def load_chunk(c):
                name, n, _ = chunks[c]
                src = {"in": w_in, "conv": conv_proj, "ret": ret_proj, "out": w_out, "q": peer_wq}[name]
                slot = chunk_slot[c]
                if holds[c] > 1:
                    wait_unit(sp, *last_of[chunks[max(b for b in range(c) if chunk_slot[b] == slot)]])
                elif slot == EXTRA:
                    wait_unit(sp, "pv", HEADS - 1, NT - 1)
                dst = (raw_tensors[slot] if c < IN_CHUNKS else W[slot])[:, :]
                if name == "conv":
                    dst, src = dst.rearrange("p (k n) -> p k n", k=CT), src
                else:
                    dst, src = dst.rearrange("p (k n) -> p k n", k=KD), src[:, n * N:(n + 1) * N]
                sp.dma_start(dst, src.rearrange("(k p) n -> p k n", p=P)).then_inc(w_in_slot[slot], 16)

            for dst, src in ((cosv, cosine), (sinv, sine), (dk, decay), (cw, conv_w), (cb, conv_b), (lg, ln_g), (lb, ln_b)):
                sp.dma_start(dst, src).then_inc(tables_in, 16)
            sp.dma_start(g2, ffn_g.partition_broadcast(P)).then_inc(g2_in, 16)
            for c in range(1, len(chunks)):
                if chunks[c] == ("out", 1, 0):
                    wait_unit(sp, "gr", 1, 0)
                    sp.wait_ge(x_kept, 1)
                    sp.dma_start(X, x.rearrange("(t p) d -> p t d", p=P)).then_inc(x_again, 16)
                load_chunk(c)
                name, n, turn = chunks[c]
                if name == "q":
                    load = 4 * turn + n
                    if load >= 2:
                        wait_unit(sp, *[("s0", 2 * load - 3), ("s", 4 * (load - 6) + 3)][load >= 6])
                    sp.dma_start(key_t[:, load % 2, :, :], keys[:, 4 * n:4 * n + 4, :]).then_inc(key_in[load % 2], 16)
            sp.wait_ge(xn2_ready, NT)
            sp.dma_start(g2, final_g.partition_broadcast(P)).then_inc(g_final_in, 16)
            for t in range(NT):
                sp.wait_ge(y_out, t + 1)
                sp.dma_start(out[t * P:(t + 1) * P, :], xn2[:, t, :]).then_inc(stored, 16)
            sp.wait_ge(stored, 16 * NT)

        @block.tensor
        def _(pe):
            def open_bank(stage, i, j=0):
                _, bank, before, _ = plan[stage, i, j]
                if before:
                    wait_emptied(pe, *before)
                return banks[bank]

            def product(out_ap, pairs):
                for n, (lhs, rhs) in enumerate(pairs):
                    last = nc.tensor.matmul(out_ap, lhs, rhs, start=n == 0, stop=n == len(pairs) - 1)
                return last

            def transpose_tile(stage, t, src):
                for half in range(2):
                    bank = open_bank(stage, t, half)
                    for i in range(4):
                        k = 4 * half + i
                        last = nc.tensor.transpose(bank[:, i * P:(i + 1) * P], src[:, k * P:(k + 1) * P], ident)
                    last.then_inc(unit_done, 1)

            def products(highs, lows):
                return [(highs[0], highs[1]), (highs[0], lows[1]), (lows[0], highs[1])]

            def channels_first(stage, c, cuts):
                for m in range(4):
                    p = 2 * c + m // 2
                    pe.wait_ge(wlo_ready, p + 1)
                    _, high, low = piece(p)
                    cols = slice(m % 2 * P, (m % 2 + 1) * P)
                    for j, (a, b) in enumerate(cuts):
                        bank = open_bank(stage, m, j)
                        if (stage, m) == ("b", 0):
                            wait_emptied(pe, "xT", 2 * (j + 1), 1)
                        product(bank[:, 0:b - a], [pair for k in range(KD) for pair in products(
                            (high[:, k, cols], xhi[:, k, a:b]), (low[:, k, cols], xlo[:, k, a:b]))]).then_inc(unit_done, 1)

            def project(stage, i, c, tiles):
                for half in range(2):
                    p = 2 * c + half
                    pe.wait_ge(wlo_ready, p + 1)
                    _, high, low = piece(p)
                    for t in tiles:
                        if half == 0:
                            open_bank(stage, i, t)
                        bank = banks[plan[stage, i, t][1]]
                        a = max(0, META + (t - 1) * P) if stage == "v" else META + t * P
                        for k in range(KD // 2):
                            K = half * (KD // 2) + k
                            pairs = products((xhi[:, K, a:a + P], high[:, k, :]), (xlo[:, K, a:a + P], low[:, k, :]))
                            for n, (lhs, rhs) in enumerate(pairs):
                                last = nc.tensor.matmul(bank, lhs, rhs, start=K == 0 and n == 0, stop=K == KD - 1 and n == 2)
                        if half:
                            last.then_inc(unit_done, 1)
                    if half == 0:
                        last.then_inc(half_used, 1)

            def tokens_first(stage, i, name, n, lhs_of, tiles, cut=None, turn=0):
                w = wait_chunk(pe, name, n, turn)
                for t in tiles:
                    bank = open_bank(stage, i, t)
                    lhs = lhs_of(t)
                    kd = len(lhs)
                    cols = slice(0, N) if cut is None else cut
                    product(bank[0:lhs[0].shape[1], :], [(lhs[k], w[:, k, cols]) for k in range(kd)]).then_inc(unit_done, 1)

            pe.wait_ge(ident_in, 16)
            pe.wait_ge(normed, 1)
            bank = open_bank("xT", 0)
            for k in range(KD):
                last = nc.tensor.transpose(bank[:, k * META:(k + 1) * META], meta_t[0:META, k * P:(k + 1) * P], ident[0:META, 0:META])
            last.then_inc(unit_done, 1)
            for t in range(NT):
                pe.wait_ge(normed, t + 2)
                transpose_tile("xT", t + 1, X[:, t, :])
            channels_first("b", 0, spans)
            channels_first("a", 1, spans)
            channels_first("q", 2, [(META, L)])
            channels_first("k", 3, spans)
            for n in range(2):
                project("v", n, 4 + n, range(NT + 1))
            for n in range(2):
                project("g", n, 6 + n, range(NT))

            key_tiles = [(0, META)] + [(META + t * P, P) for t in range(NT)]
            wait_emptied(pe, "v", 1, NT)
            for h in range(HEADS + 1):
                if h < HEADS:
                    wait_emptied(pe, "k", h, 1)
                    for j, (a, rows) in enumerate(key_tiles):
                        first = 0 if j == 0 else (j - 1) * P
                        bank = open_bank("sc", h, j)
                        nc.tensor.matmul(bank[0:rows, 0:T - first], k_t[:, h, a:a + rows], q_t[:, h, first:T], start=True, stop=True).then_inc(unit_done, 1)
                if h > 0:
                    g = h - 1
                    pe.wait_ge(p_ready, (NT + 1) * h)
                    for i in range(NT):
                        bank = open_bank("pv", g, i)
                        pairs = [(p_buf[0:META, g % 2, i * P:(i + 1) * P], v_meta[0:META, g * DV:(g + 1) * DV])]
                        for j in range(i + 1):
                            a = p_at[j + 1] + (i - j) * P
                            pairs.append((p_buf[:, g % 2, a:a + P], v_x[:, j, g * DV:(g + 1) * DV]))
                        product(bank[:, 0:DV], pairs).then_inc(unit_done, 1)

            project("gr", 0, 8, range(1))
            project("gc", 0, 9, range(NT))
            pe.wait_ge(conv_done, CT)
            bank = open_bank("mean", 0)
            product(bank, [(ones, cv[:, c, :]) for c in range(CT)]).then_inc(unit_done, 1)
            project("gc", 1, 10, range(NT))
            pe.wait_ge(squared, CT)
            bank = open_bank("var", 0)
            product(bank, [(ones, squares[:, c, :]) for c in range(CT)]).then_inc(unit_done, 1)
            project("gr", 1, 11, range(1))

            pe.wait_ge(og_done, HEADS * NT)
            transpose_tile("oT", 0, big_a[:, 0, :])

            def conv_cols(t):
                return [cv[:, c, t * P:(t + 1) * P] for c in range(CT)]

            def o_cols(t):
                return [oT[:, k, t * P:(t + 1) * P] for k in range(KD)]

            def m_cols(t):
                return [m_rest[:, k, (t - 1) * P:t * P] if t else m_first[:, k, :] for k in range(KD)]

            def pe_unit(stage, i, j, turn):
                if stage == "cp":
                    pe.wait_ge(conv_act, CT)
                    tokens_first("cp", i, "conv", 0, conv_cols, [j], slice(i * N, (i + 1) * N), turn)
                elif stage == "gr":
                    tokens_first("gr", i, "in", 10 + i, lambda t: [x_rest[:, k, (t - 1) * P:t * P] for k in range(KD)], [j], None, turn)
                elif stage == "rp":
                    wait_emptied(pe, "oT", j, 1)
                    tokens_first("rp", i, "ret", i, o_cols, [j], None, turn)
                elif stage == "mT":
                    if j == 0:
                        pe.wait_ge(merged, 2 * NT if i else 2)
                        transpose_tile("mT", i, rest_b[:, i - 1, :] if i else big_b[:, 0, :])
                elif stage == "wo":
                    wait_emptied(pe, "mT", j, 1)
                    tokens_first("wo", i, "out", i, m_cols, [j], None, turn)
                elif stage == "zT":
                    if j == 0:
                        pe.wait_ge(xn2_ready, i + 1)
                        transpose_tile("zT", i, xn2[:, i, :])
                elif stage == "wq":
                    wait_emptied(pe, "zT", NT - 1, 1)
                    w, m = wait_chunk(pe, "q", i // 4, 1), i % 4
                    bank = open_bank("wq", i)
                    product(bank[:, 0:3 * P], [(w[:, k, m * P:(m + 1) * P], oT[:, k, P:T]) for k in range(KD)]).then_inc(unit_done, 1)
                elif stage == "s":
                    wait_emptied(pe, "wq", i)
                    load = 4 + i // 4
                    pe.wait_ge(key_in[load % 2], 16 * (load // 2 + 1))
                    bank = open_bank("s", i)
                    for t in range(3):
                        last = nc.tensor.matmul(bank[:, t * NK:(t + 1) * NK], q_top[:, i % 2, t * P:(t + 1) * P], key_t[:, load % 2, i % 4, :], start=True, stop=True)
                    last.then_inc(unit_done, 1)

            for stage, j in (("rp", 0), ("cp", 0)):
                for n in range(2):
                    pe_unit(stage, n, j, 0)
            pe_unit("mT", 0, 0, 0)
            for n in range(2):
                pe_unit("wo", n, 0, 0)
            for t in REST:
                transpose_tile("oT", t, big_a[:, t, :])
            pe_unit("zT", 0, 0, 0)
            wait_emptied(pe, "zT", 0, 1)
            for h in range(PH + 1):
                if h < PH:
                    w = wait_chunk(pe, "q", h // 2)
                    bank = open_bank("wq0", h)
                    for side in range(2):
                        m = h % 2 * 2 + side
                        last = product(bank[:, side * P:(side + 1) * P], [(w[:, k, m * P:(m + 1) * P], oT[:, k, 0:P]) for k in range(KD)])
                    last.then_inc(unit_done, 1)
                if h > 0:
                    g = h - 1
                    load = g // 2
                    wait_emptied(pe, "wq0", g)
                    pe.wait_ge(key_in[load % 2], 16 * (load // 2 + 1))
                    bank = open_bank("s0", g)
                    for side in range(2):
                        last = nc.tensor.matmul(bank[:, side * NK:(side + 1) * NK], q_top[:, g % 2, side * P:(side + 1) * P],
                                                key_t[:, load % 2, g % 2 * 2 + side, :], start=True, stop=True)
                    last.then_inc(unit_done, 1)

            y = [banks[0], banks[1]]
            for before in plan["before the sum"]:
                wait_emptied(pe, *before)

            def open_sum(t):
                pe.wait_ge(y_copied, t * 2 + 1)
                for n in range(2):
                    nc.tensor.matmul(y[n], ident, X_flat[:, bass.ds(t * D + n * N, N)], start=True, stop=False)

            def add_row(group, k):
                pe.wait_ge(diag_ready, group * TOP + (k + 1))
                pe.wait_ge(v_in[k % SLOTS], group * (16 * TOP // SLOTS) + 16 * (k // SLOTS + 1))
                for n in range(2):
                    last = nc.tensor.matmul(y[n], diag[:, k % SLOTS, :], v_ring[:, k % SLOTS, n * N:(n + 1) * N], start=False, stop=False)
                last.then_inc(v_used, 1)

            def close_sum():
                for n in range(2):
                    last = nc.tensor.matmul(y[n][:, 0:2], zeros, zeros[:, 0:2], start=False, stop=True)
                last.then_inc(y_done, 1)

            open_sum(0)
            for place in range(-1, 2 * PH * TOP):
                if place == PH * TOP:
                    close_sum()
                    open_sum(1)
                if place >= 0:
                    add_row(place // TOP, place % TOP)
                for at, kind, stage, i, j, _ in steps_beside:
                    if at == place and kind == "unit":
                        pe_unit(stage, i, j, 1)
            close_sum()
            with pe.Fori(2, NT) as t:
                open_sum(t)
                with pe.Fori(0, PH // 2) as half:
                    for k in range(2 * TOP):
                        add_row(t * PH + half * 2, k)
                close_sum()

        @block.scalar
        def _(act):
            A = nc.scalar.activation
            roots = [0]

            def rms(src, junk, at, count, ready, rows=P):
                roots[0] += 1
                column = stat[0:rows, at:at + 1]
                A(junk, src, ACT.Square, accum_out=column).then_inc(act_step, 1)
                act.wait_ge(act_step, roots[0])
                A(column, column, ACT.Sqrt, scale=1.0 / count, bias=eps[0:rows, :]).then_inc(ready, 1)

            act.wait_ge(consts_set, 1)
            act.wait_ge(x_in, 16)
            rms(meta_t[0:META, :], tmp_wide[0:META, :], 0, D, ssq_ready, META)
            for t in range(NT - 1):
                act.wait_ge(x_tile_in[t], 16)
                rms(X[:, t, :], tmp_wide, t + 1, D, ssq_ready)

            def empty(stage, i, j, dst, shape=None, func=ACT.Copy):
                bank = wait_unit(act, stage, i, j)
                src = bank[0:dst.shape[0], :] if shape is None else shape(bank)
                A(dst, src, func).then_inc(emptied["act"], 1)

            def high_part(p):
                if p >= PIECES:
                    return
                raw, high, _ = piece(p)
                if p == 0:
                    act.wait_ge(first_piece_in, 16)
                elif p == 1 or p % 2 == 0:
                    act.wait_ge(w_in_slot[p // 2 % WSLOTS], 16 * (p // 2 // WSLOTS + 1))
                if p == 1:
                    wait_unit(act, "xT", 0, 0)
                    act.wait_ge(normed, NT + 1)
                elif p == AFTER_RETENTION:
                    wait_emptied(act, "sc", HEADS - 1, NT)
                elif p >= 2:
                    before = max(q for q in range(p) if high_place[q] == high_place[p])
                    c = before // 2
                    if before % 2:
                        wait_unit(act, *last_of[chunks[c]])
                    elif c < BY_COLUMNS:
                        stage = last_of[chunks[c]][0]
                        wait_unit(act, stage, 1, 0 if stage == "q" else 1)
                    else:
                        act.wait_ge(half_used, c - BY_COLUMNS + 1)
                A(high, raw, ACT.Copy).then_inc(whi_ready, 1)

            bank = wait_unit(act, "xT", 0, 0)
            A(xhi[:, :, 0:META], bank[:, 0:KD * META].rearrange("p (k t) -> p k t", k=KD), ACT.Copy).then_inc(xhi_ready, 1)
            A(meta_whole, bank[:, 0:KD * META].rearrange("p (k t) -> p k t", k=KD), ACT.Copy).then_inc(emptied["act"], 1)
            four = lambda b: b[:, :].rearrange("p (k t) -> p k t", k=4)
            for t in range(NT):
                if t == NT - 1:
                    act.wait_ge(x_tile_in[t], 16)
                    rms(X[:, t, :], tmp_wide, t + 1, D, ssq_ready)
                    high_part(0)
                for i in range(2):
                    bank = wait_unit(act, "xT", t + 1, i)
                    A(xhi[:, 4 * i:4 * i + 4, META + t * P:META + (t + 1) * P], four(bank), ACT.Copy).then_inc(xhi_ready, 1)
            high_part(1)
            for c in range(CT):
                for i, (a, b) in enumerate(spans):
                    empty("b", c, i, sig_b[:, c, a:b], lambda bank: bank[:, 0:HALF], ACT.Sigmoid)
                if c % 2:
                    high_part(2 + c // 2)
            for p in (4, 5):
                high_part(p)
            swaps = [("q", h, 0, T) for h in range(HEADS)] + [("k", h, i, HALF) for h in range(HEADS) for i in range(2)]
            for n, (stage, h, i, width) in enumerate(swaps):
                bank = wait_unit(act, stage, h, i)
                if n >= 2:
                    act.wait_ge(swap_used, n - 1)
                A(tmp[0:64, n % 2, 0:width], bank[64:128, 0:width], ACT.Copy).then_inc(swapped, 1)
                A(tmp[64:128, n % 2, 0:width], bank[0:64, 0:width], ACT.Copy).then_inc(swapped, 1)
                if h % 2 and (stage == "q" or i):
                    high_part((6 if stage == "q" else 8) + h // 2)
            for n in range(2):
                high_part(10 + 2 * n)
                for t in range(NT + 1):
                    dst = v_x[:, t - 1, n * N:(n + 1) * N] if t else v_meta[0:META, n * N:(n + 1) * N]
                    empty("v", n, t, dst)
                high_part(11 + 2 * n)
            for n in range(2):
                high_part(14 + 2 * n)
                for t in range(NT):
                    bank = wait_unit(act, "g", n, t)
                    u = n * NT + t
                    if u >= 2:
                        act.wait_ge(gsig_used, u - 1)
                    A(tmp[:, 2 + u % 2, :], bank, ACT.Sigmoid).then_inc(gsig_ready, 1)
                high_part(15 + 2 * n)
            for h in range(HEADS):
                for i in range(NT):
                    bank = wait_unit(act, "pv", h, i)
                    u = h * NT + i
                    rms(bank[:, 0:DV], tmp[:, 0, 0:DV], 8 + u, DV, pv_ssq)
            for p in (18, 19, 20):
                high_part(p)
            empty("gr", 0, 0, big_c[:, 0, 0:N], None, ACT.Sigmoid)
            for p in (21, 22):
                high_part(p)
            for t in range(NT):
                empty("gc", 0, t, big_b[:, t, 0:N], None, ACT.Sigmoid)
            for c in range(CT):
                act.wait_ge(centered, c + 1)
                A(squares[:, c, :], cv[:, c, :], ACT.Square).then_inc(squared, 1)
            high_part(23)
            for t in range(NT):
                empty("gc", 1, t, big_b[:, t, N:D], None, ACT.Sigmoid)
            wait_emptied(act, "var", 0)
            A(tmp[:, 0, :], tmp[:, 0, :], ACT.Sqrt).then_inc(root_ready, 1)
            empty("gr", 1, 0, big_c[:, 0, N:D], None, ACT.Sigmoid)
            for i in range(2):
                empty("oT", 0, i, oT[:, 4 * i:4 * i + 4, 0:P], four)
            for c in range(CT):
                act.wait_ge(scaled, c + 1)
                A(squares[:, c, :], cv[:, c, :], ACT.Sigmoid, scale=lg[:, c:c + 1], bias=lb[:, c:c + 1]).then_inc(conv_sig, 1)

            def act_step_beside(kind, stage, i, j):
                if kind == "act":
                    act.wait_ge(h_ready, 2 * i + 2)
                    rms(X[:, i, :], tmp_wide, 24 + i, D, h_ssq)
                elif stage == "gr":
                    if i:
                        act.wait_ge(merged, 2 + j)
                    empty("gr", i, j, rest_gate[j - 1], None, ACT.Sigmoid)
                elif stage == "mT":
                    if i:
                        act.wait_ge(merged, 2 * NT)
                        empty("mT", i, j, m_rest[:, 4 * j:4 * j + 4, (i - 1) * P:i * P], four)
                    else:
                        empty("mT", 0, j, m_first[:, 4 * j:4 * j + 4, :], four)
                elif stage == "zT":
                    empty("zT", i, j, oT[:, 4 * j:4 * j + 4, i * P:(i + 1) * P], four)
                elif stage == "wq":
                    if i >= 2:
                        wait_unit(act, "s", i - 2)
                    empty("wq", i, 0, q_top[:, i % 2, 0:3 * P], lambda b: b[:, 0:3 * P])
                elif stage == "s":
                    empty("s", i, 0, scores_t[:, 1:NT, i, :], lambda b: b[:, 0:3 * NK].rearrange("p (t k) -> p t k", t=3))
                    if i % 2:
                        wait_emptied(act, "s", i)
                        act.sem_inc(scores_ready, 1)

            def softmax(count):
                act.wait_ge(top_ready, count)
                A(gate_exp, small["top"], ACT.Exp, bias=soft[:, 0:1], accum_out=soft[:, 1:2]).then_inc(soft_ready, 1)

            for i in range(2):
                act_step_beside("unit", "mT", 0, i)
            act_step_beside("act", "rms", 0, 0)
            for i in range(2):
                act_step_beside("unit", "zT", 0, i)
            for h in range(PH + 1):
                if h < PH:
                    if h >= 2:
                        wait_unit(act, "s0", h - 2)
                    empty("wq0", h, 0, q_top[:, h % 2, 0:2 * P], lambda b: b[:, 0:2 * P])
                if h > 0:
                    empty("s0", h - 1, 0, scores_t[:, 0, 2 * h - 2:2 * h, :], lambda b: b[:, 0:2 * NK].rearrange("p (k t) -> p k t", k=2))
                    wait_emptied(act, "s0", h - 1)
                    act.sem_inc(scores_ready, 1)
                if h == 1:
                    softmax(1)

            def tanh(group):
                act.wait_ge(arg_ready, group + 1)
                A(small["th"], small["arg"], ACT.Tanh, scale=float(np.sqrt(2 / np.pi))).then_inc(tanh_ready, 1)
                act.wait_ge(w_ready, group + 1)

            def diagonal(group, i, k):
                act.wait_ge(v_used, group * TOP + (k + 1))
                A(diag[:, k % SLOTS, :], ident, ACT.Copy, scale=weights[:, i * TOP + k:i * TOP + k + 1]).then_inc(diag_ready, 1)

            def copy_sum(t):
                act.wait_ge(y_done, t + 1)
                for n in range(2):
                    A(X_flat[:, bass.ds(t * D + n * N, N)], banks[n], ACT.Copy).then_inc(y_copied, 1)

            def final_root(t):
                act.wait_ge(y_copied, t * 2 + 3)
                act.wait_ge(tile_set, t + 1)
                A(xn2_flat[:, bass.ds(t * D, D)], X_flat[:, bass.ds(t * D, D)], ACT.Square, accum_out=stat[:, 40:41]).then_inc(fin_step, 1)
                act.wait_ge(fin_step, t + 1)
                A(stat[:, 41:42], stat[:, 40:41], ACT.Sqrt, scale=1.0 / D, bias=eps).then_inc(fin_ssq, 1)

            for h in range(2 * PH):
                if h == PH:
                    copy_sum(0)
                    final_root(0)
                tanh(h)
                for k in range(TOP):
                    diagonal(h, h % 2, k)
                    for at, kind, stage, i, j, owner in steps_beside:
                        if at // TOP == h and min(at % TOP + 8, TOP - 1) == k and (kind == "act" or owner == "act"):
                            act_step_beside(kind, stage, i, j)
                softmax(h + 2)
            copy_sum(1)
            with act.Fori(2, NT) as t:
                act.wait_ge(y_out, t - 1)
                final_root(t - 1)
                with act.Fori(0, PH // 2) as half:
                    for i in range(2):
                        group = t * PH + half * 2 + i
                        tanh(group)
                        for k in range(TOP):
                            diagonal(group, i, k)
                        softmax(group + 2)
                copy_sum(t)
            act.wait_ge(y_out, NT - 1)
            final_root(NT - 1)

        @block.vector
        def _(dve):
            TT, TS, STT = nc.vector.tensor_tensor, nc.vector.tensor_scalar, nc.vector.scalar_tensor_tensor
            steps = [0]

            def link(ins):
                steps[0] += 1
                ins.then_inc(dve_step, 1)
                dve.wait_ge(dve_step, steps[0])

            nc.vector.memset(zeros, 0.0)
            nc.vector.memset(eps, EPS)
            nc.vector.memset(ones, 1.0 / CONV)
            nc.vector.memset(hb[:, :, 0:PAD], 0.0).then_inc(consts_set, 1)
            dve.wait_ge(consts_set, 1)

            dve.wait_ge(g1_in, 16)
            dve.wait_ge(ssq_ready, 1)
            link(nc.vector.reciprocal(stat[0:META, 0:1], stat[0:META, 0:1]))
            STT(meta_t[0:META, :], meta_t[0:META, :], stat[0:META, 0:1], g1[0:META, :], ALU.mult, ALU.mult).then_inc(normed, 1)
            for t in range(NT):
                dve.wait_ge(ssq_ready, t + 2)
                link(nc.vector.reciprocal(stat[:, t + 1:t + 2], stat[:, t + 1:t + 2]))
                STT(X[:, t, :], X[:, t, :], stat[:, t + 1:t + 2], g1, ALU.mult, ALU.mult).then_inc(normed, 1)

            wait_emptied(dve, "xT", 0, 0)
            wait_unit(dve, "xT", NT, 1)
            dve.wait_ge(xhi_ready, 1)
            nc.vector.tensor_tensor(xlo[:, :, 0:META], meta_whole, xhi[:, :, 0:META], ALU.subtract)
            for t in range(NT):
                for i in range(2):
                    bank = wait_unit(dve, "xT", t + 1, i)
                    dve.wait_ge(xhi_ready, 2 * t + i + 2)
                    place = (slice(None), slice(4 * i, 4 * i + 4), slice(META + t * P, META + (t + 1) * P))
                    TT(xlo[place], bank.rearrange("p (k t) -> p k t", k=4), xhi[place], ALU.subtract).then_inc(emptied["dve"], 1)

            dve.wait_ge(tables_in, 16 * 7)
            for c in range(CT):
                for i, (a, b) in enumerate(spans):
                    wait_emptied(dve, "b", c, i)
                    bank = wait_unit(dve, "a", c, i)
                    TT(hb[:, c, PAD + a:PAD + b], bank[:, 0:HALF], sig_b[:, c, a:b], ALU.mult).then_inc(emptied["dve"], 1)

            def rotate(n, stage, h, i, dst, a, b):
                bank = wait_unit(dve, stage, h, i)
                dve.wait_ge(swapped, 2 * (n + 1))
                link(TT(dst, bank[:, 0:b - a], cosv[:, a:b], ALU.mult))
                link(TT(tmp[:, n % 2, 0:b - a], tmp[:, n % 2, 0:b - a], sinv[:, a:b], ALU.mult))
                TT(dst, dst, tmp[:, n % 2, 0:b - a], ALU.add).then_inc(emptied["dve"], 1)
                wait_emptied(dve, stage, h, i)
                dve.sem_inc(swap_used, 1)

            def convolve(c):
                link(TS(cv[:, c, :], hb[:, c, 0:T], cw[:, c, 0:1], cb[:, c:c + 1], ALU.mult, ALU.add))
                for w in range(1, TAPS):
                    ins = STT(cv[:, c, :], hb[:, c, w:w + T], cw[:, c, w:w + 1], cv[:, c, :], ALU.mult, ALU.add)
                    if w < TAPS - 1:
                        link(ins)
                ins.then_inc(conv_done, 1)

            for h in range(HEADS):
                rotate(h, "q", h, 0, q_t[:, h, :], META, L)
            n = HEADS
            for h in range(HEADS):
                for i, (a, b) in enumerate(spans):
                    rotate(n, "k", h, i, k_t[:, h, a:b], a, b)
                    n += 1
            wait_emptied(dve, "a", CT - 1, 1)
            for c in range(CT - 1):
                convolve(c)
            for n in range(2):
                for t in range(NT):
                    u = n * NT + t
                    bank = wait_unit(dve, "g", n, t)
                    dve.wait_ge(gsig_ready, u + 1)
                    TT(big_a[:, t, n * N:(n + 1) * N], bank, tmp[:, 2 + u % 2, :], ALU.mult).then_inc(emptied["dve"], 1)
                    wait_emptied(dve, "g", n, t)
                    dve.sem_inc(gsig_used, 1)

            for h in range(HEADS + 1):
                if h < HEADS:
                    if h >= 2:
                        wait_unit(dve, "pv", h - 2, NT - 1)
                    for j in range(NT + 1):
                        bank = wait_unit(dve, "sc", h, j)
                        rows, first, d0 = (META, 0, META) if j == 0 else (P, (j - 1) * P, 0)
                        a = p_at[j]
                        TT(p_buf[0:rows, h % 2, a:a + T - first], bank[0:rows, 0:T - first], dk[0:rows, h, d0:d0 + T - first], ALU.mult).then_inc(emptied["dve"], 1)
                        wait_emptied(dve, "sc", h, j)
                        dve.sem_inc(p_ready, 1)
                if h > 0:
                    g = h - 1
                    for i in range(NT):
                        u = g * NT + i
                        bank = wait_unit(dve, "pv", g, i)
                        dve.wait_ge(pv_ssq, u + 1)
                        link(nc.vector.reciprocal(stat[:, 8 + u:9 + u], stat[:, 8 + u:9 + u]))
                        cols = big_a[:, i, g * DV:(g + 1) * DV]
                        STT(cols, bank[:, 0:DV], stat[:, 8 + u:9 + u], cols, ALU.mult, ALU.mult).then_inc(emptied["dve"], 1)
                        wait_emptied(dve, "pv", g, i)
                        dve.sem_inc(og_done, 1)

            convolve(CT - 1)

            bank = wait_unit(dve, "mean", 0)
            dve.wait_ge(conv_done, CT)
            for c in range(CT):
                ins = TT(cv[:, c, :], cv[:, c, :], bank, ALU.subtract)
                ins.then_inc(centered, 1)
            dve.wait_ge(centered, CT)
            dve.sem_inc(emptied["dve"], 1)
            bank = wait_unit(dve, "var", 0)
            TS(tmp[:, 0, :], bank, EPS, None, ALU.add).then_inc(emptied["dve"], 1)
            dve.wait_ge(root_ready, 1)
            link(nc.vector.reciprocal(tmp[:, 1, :], tmp[:, 0, :]))
            for c in range(CT):
                dve.wait_ge(squared, c + 1)
                TT(cv[:, c, :], cv[:, c, :], tmp[:, 1, :], ALU.mult).then_inc(scaled, 1)
            for c in range(CT):
                dve.wait_ge(conv_sig, c + 1)
                link(TS(cv[:, c, :], cv[:, c, :], lg[:, c:c + 1], lb[:, c:c + 1], ALU.mult, ALU.add))
                TT(cv[:, c, :], cv[:, c, :], squares[:, c, :], ALU.mult).then_inc(conv_act, 1)

            wait_unit(dve, "gr", 1, 0)
            dve.wait_ge(conv_act, CT)
            TT(x_rest, xhi[:, :, META + P:L], xlo[:, :, META + P:L], ALU.add).then_inc(x_kept, 1)

            def dve_step_beside(kind, stage, i, j):
                cols = slice(i * N, (i + 1) * N)
                if stage in ("cp", "rp"):
                    gate_b, gate_c = (rest_b[:, j - 1, cols], rest_gate[j - 1]) if j else (big_b[:, 0, cols], big_c[:, 0, cols])
                    if stage == "rp":
                        wait_emptied(dve, "gr", i, j)
                    bank = wait_unit(dve, stage, i, j)
                    gate = gate_b if stage == "cp" else gate_c
                    TT(gate, bank, gate, ALU.mult).then_inc(emptied["dve"], 1)
                    if stage == ("rp" if j else "cp"):
                        wait_emptied(dve, stage, i, j)
                        TT(gate_b, gate_b, gate_c, ALU.add).then_inc(merged, 1)
                elif stage == "wo":
                    bank = wait_unit(dve, "wo", i, j)
                    TT(X[:, j, cols], bank, X[:, j, cols], ALU.add).then_inc(emptied["dve"], 1)
                    wait_emptied(dve, "wo", i, j)
                    dve.sem_inc(h_ready, 1)
                elif kind == "dve":
                    dve.wait_ge(h_ssq, i + 1)
                    dve.wait_ge(g2_in, 16)
                    link(nc.vector.reciprocal(stat[:, 24 + i:25 + i], stat[:, 24 + i:25 + i]))
                    STT(xn2[:, i, :], X[:, i, :], stat[:, 24 + i:25 + i], g2, ALU.mult, ALU.mult).then_inc(xn2_ready, 1)

            def dve_beside(places):
                for at, kind, stage, i, j, owner in steps_beside:
                    if at in places and (kind == "dve" or owner == "dve"):
                        dve_step_beside(kind, stage, i, j)

            def dve_beside_ahead(n):
                ahead = [step for step in steps_beside if step[0] == -1]
                for at, kind, stage, i, j, owner in ahead[n:n + 1]:
                    dve_step_beside(kind, stage, i, j)

            for stage in ("rp", "cp"):
                for n in range(2):
                    dve_step_beside("unit", stage, n, 0)
            dve.wait_ge(x_again, 16)
            for n in range(2):
                dve_step_beside("unit", "wo", n, 0)
            dve_step_beside("dve", "norm", 0, 0)
            for t in REST:
                for i in range(2):
                    bank = wait_unit(dve, "oT", t, i)
                    nc.vector.tensor_copy(oT[:, 4 * i:4 * i + 4, t * P:(t + 1) * P], bank.rearrange("p (k t) -> p k t", k=4)).then_inc(emptied["dve"], 1)

            def route(parity, before_idx):
                pair, rest, vals, keyf = small["pair"], small["rest"], small["vals"], small["keyf"]
                for side in range(2):
                    src = pair[:, side * NK:(side + 1) * NK]
                    v8 = [vals[:, side * TOP + 8 * i:side * TOP + 8 * i + 8] for i in range(2)]
                    i8 = [ids[:, side * TOP + 8 * i:side * TOP + 8 * i + 8] for i in range(2)]
                    chain(nc.vector.max(v8[0], src))
                    chain(nc.vector.max_index(i8[0], v8[0], src))
                    chain(nc.vector.match_replace(rest, v8[0], src, LOWEST))
                    chain(nc.vector.max(v8[1], rest))
                    chain(nc.vector.max_index(i8[1], v8[1], rest))
                chain(nc.vector.tensor_copy(keyf, ids))
                grid = pair_scores.rearrange("p (i j) -> p i j", i=TOP)
                chain(TT(grid, vals[:, 0:TOP].unsqueeze(2).broadcast_to([P, TOP, TOP]),
                         vals[:, TOP:2 * TOP].unsqueeze(1).broadcast_to([P, TOP, TOP]), ALU.add))
                top = small["top"]
                chain(nc.vector.max(top[:, 0:8], pair_scores))
                chain(nc.vector.max_index(pos[:, 0:8], top[:, 0:8], pair_scores))
                chain(nc.vector.match_replace(rest2, top[:, 0:8], pair_scores, LOWEST))
                chain(nc.vector.max(top[:, 8:16], rest2))
                chain(TS(soft[:, 0:1], top[:, 0:1], -1.0, None, ALU.mult))
                dve.sem_inc(top_ready, 1)
                chain(nc.vector.max_index(pos[:, 8:16], top[:, 8:16], rest2))
                chain(TS(pos[:, TOP:2 * TOP], pos[:, 0:TOP], 4, None, ALU.logical_shift_right))
                chain(TS(pos[:, 2 * TOP:3 * TOP], pos[:, 0:TOP], TOP - 1, None, ALU.bitwise_and))
                chain(nc.vector.tensor_copy(small["posf"], pos[:, TOP:3 * TOP]))
                hot3 = hot.rearrange("p (k j) -> p k j", k=TOP)
                for side in range(2):
                    place = small["posf"][:, side * TOP:(side + 1) * TOP].unsqueeze(2).broadcast_to([P, TOP, TOP])
                    chain(TT(hot3, place, small["iota"].unsqueeze(1).broadcast_to([P, TOP, TOP]), ALU.is_equal))
                    chain(TT(hot3, hot3, keyf[:, side * TOP:(side + 1) * TOP].unsqueeze(1).broadcast_to([P, TOP, TOP]), ALU.mult))
                    chain(nc.vector.tensor_reduce(small["chosen"][:, side * TOP:(side + 1) * TOP], hot3, AX.X, ALU.add))
                before_idx()
                chain(STT(experts[:, parity * TOP:(parity + 1) * TOP], small["chosen"][:, 0:TOP], float(NK), small["chosen"][:, TOP:2 * TOP], ALU.mult, ALU.add))
                dve.sem_inc(idx_ready, 1)

            chained = [0]

            def chain(ins):
                chained[0] += 1
                ins.then_inc(group_step, 1)
                dve.wait_ge(group_step, chained[0])

            link(nc.vector.memset(scores[:, GROUPS * 2 * NK:(GROUPS + 1) * 2 * NK], 0.0))
            nc.vector.memset(small["gate"], 0.0).then_inc(u_used, SLOTS)
            dve.sem_inc(v_used, SLOTS)
            dve.sem_inc(y_copied, 1)
            dve.wait_ge(u_used, SLOTS)
            dve.wait_ge(iota_set, 1)
            dve.wait_ge(scores_ready, 1)
            chain(nc.vector.tensor_copy(small["pair"], scores[:, 0:2 * NK]))
            route(0, lambda: None)

            def load_tile(t):
                nc.vector.tensor_copy(x_cur, xn2_flat[:, bass.ds(t * D, D)]).then_inc(tile_set, 1)

            def dot(group, k):
                dve.wait_ge(u_in[k % SLOTS], group * (16 * TOP // SLOTS) + 16 * (k // SLOTS + 1))
                nc.vector.tensor_tensor_reduce(out=junk, in0=u_ring[:, k % SLOTS, :], in1=x_cur, scale=1.0, scalar=0.0,
                                               op0=ALU.mult, op1=ALU.add, accum_out=small["act"][:, k:k + 1]).then_inc(u_used, 1)
                dve.wait_ge(u_used, group * TOP + (SLOTS + k + 1))

            def weigh(group, i):
                dots, arg = small["act"], small["arg"]
                chain(TT(arg, dots, dots, ALU.mult))
                chain(TS(arg, arg, 0.044715, 1.0, ALU.mult, ALU.add))
                chain(TT(arg, arg, dots, ALU.mult))
                dve.sem_inc(arg_ready, 1)
                dve.wait_ge(soft_ready, group + 1)
                chain(nc.vector.reciprocal(soft[:, 2:3], soft[:, 1:2]))
                chain(TS(small["gate"], gate_exp, soft[:, 2:3], 0.5, ALU.mult, ALU.mult))
                dve.wait_ge(tanh_ready, group + 1)
                chain(STT(arg, small["th"], 1.0, dots, ALU.add, ALU.mult))
                chain(TT(weights[:, i * TOP:(i + 1) * TOP], arg, small["gate"], ALU.mult))
                dve.sem_inc(w_ready, 1)

            def route_next(group, i):
                chain(nc.vector.tensor_copy(small["pair"], scores[:, bass.ds(group * 2 * NK + 2 * NK, 2 * NK)]))
                route(1 - i, lambda: dve.wait_ge(v_used, group * TOP + SLOTS))

            def restart_chain():
                dve.sem_clear(group_step)
                chained[0] = 0

            def final_norm(t):
                dve.wait_ge(fin_ssq, t + 1)
                chain(nc.vector.reciprocal(stat[:, 42:43], stat[:, 41:42]))
                STT(xn2_flat[:, bass.ds(t * D, D)], X_flat[:, bass.ds(t * D, D)], stat[:, 42:43], g2, ALU.mult, ALU.mult).then_inc(y_out, 1)

            load_tile(0)
            dve.wait_ge(tile_set, 1)
            dve.wait_ge(gates_moved, 1)
            for h in range(2 * PH):
                if h == PH:
                    load_tile(1)
                restart_chain()
                if h == PH:
                    dve.wait_ge(tile_set, 2)
                for k in range(TOP):
                    dot(h, k)
                    if h == 0 and k % 2:
                        dve_beside_ahead(k // 2)
                    elif h > 0 and k % 2:
                        dve_beside([(h - 1) * TOP + 8 + k // 2])
                weigh(h, h % 2)
                if h + 1 < 2 * PH:
                    dve.wait_ge(scores_ready, h + 2)
                route_next(h, h % 2)
                dve_beside(range(h * TOP, h * TOP + 8))
            dve.wait_ge(g_final_in, 16)
            final_norm(0)
            with dve.Fori(2, NT) as t:
                load_tile(t)
                with dve.Fori(0, PH // 2) as half:
                    for i in range(2):
                        group = t * PH + half * 2 + i
                        restart_chain()
                        dve.wait_ge(tile_set, t + 1)
                        for k in range(TOP):
                            dot(group, k)
                        weigh(group, i)
                        route_next(group, i)
                restart_chain()
                final_norm(t - 1)

            restart_chain()
            final_norm(NT - 1)

        @block.gpsimd
        def _(pool):
            for p in range(PIECES):
                raw, high, low = piece(p)
                pool.wait_ge(whi_ready, p + 1)
                nc.gpsimd.tensor_tensor(low, raw, high, ALU.subtract).then_inc(wlo_ready, 1)
            wait_emptied(pool, "g", 1, NT - 1)
            nc.gpsimd.iota(small["iota"], pattern=[[1, TOP]], base=0, channel_multiplier=0, allow_small_or_imprecise_dtypes=True).then_inc(iota_set, 1)
            wait_emptied(pool, "gc", 1, NT - 1)
            wait_unit(pool, "gr", 1, 0)
            pool.wait_ge(conv_act, CT)
            pool.wait_ge(x_kept, 1)
            nc.gpsimd.tensor_copy(rest_b, big_b[:, 1:NT, :]).then_inc(gates_moved, 1)
            pool.wait_ge(gates_moved, 1)
            wait_unit(pool, "oT", NT - 1, 1)
            with pool.Fori(0, GROUPS, 2) as group:
                for i in range(2):
                    pool.wait_ge(idx_ready, group + (i + 1))
                    for table, ring, arrived, used in ((peer_u, u_ring, u_in, u_used), (peer_v, v_ring, v_in, v_used)):
                        for k in range(TOP):
                            pool.wait_ge(used, group * TOP + (i * TOP + k + 1))
                            pool.sem_inc(slots_found, 1)
                            pool.indirect_dma_start(ring[:, k % SLOTS, :], None, table,
                                                    bass.IndirectOffsetOnAxis(experts[:, i * TOP + k:i * TOP + k + 1], 0)).then_inc(arrived[k % SLOTS], 16)


_NAMES = ["x", "meta", "w_in", "conv_w", "conv_b", "ln_g", "ln_b", "conv_proj", "ret_proj", "w_out", "mix_g", "ffn_g",
          "final_g", "peer_wq", "keys", "peer_u", "peer_v", "cosine", "sine", "decay", "identity"]


def _tables():
    half = P // 2
    freqs = np.float32(10000.0) ** (-np.arange(half, dtype=np.float32) / np.float32(half))
    angle = np.arange(L, dtype=np.float32)[None, :] * freqs[:, None]
    cosine = np.concatenate([np.cos(angle)] * 2).astype(np.float32)
    sine = np.concatenate([-np.sin(angle), np.sin(angle)]).astype(np.float32)
    log_gamma = np.log(1.0 - 2.0 ** (-5.0 - np.arange(HEADS)))
    distance = np.arange(L)[None, None, :] - np.arange(P)[:, None, None]
    decay = np.where(distance >= 0, np.exp(log_gamma[None, :, None] * np.maximum(distance, 0)), 0.0) * P ** -0.5
    return {"cosine": cosine, "sine": sine, "decay": decay.astype(np.float32), "identity": np.eye(P, dtype=np.float32)}


def kernel(x, meta_tokens, norm_mix_g, w_in, conv_dw_w, conv_dw_b, conv_ln_g, conv_ln_b, conv_proj_w, ret_proj_w,
           w_out, norm_ffn_g, peer_w_q, peer_sub_keys, peer_u, peer_v, norm_final_g):
    import concourse.bacc as bacc
    from concourse.bass_utils import run_bass_kernel_spmd

    def channels(a):
        return np.moveaxis(np.asarray(a).reshape(-1, CT, P), (2, 1), (0, 1))

    given = {
        "x": np.asarray(x)[0], "meta": np.asarray(meta_tokens), "w_in": np.asarray(w_in)[0],
        "conv_w": channels(np.asarray(conv_dw_w)[0]),
        "conv_b": channels(conv_dw_b[0])[:, :, 0], "ln_g": channels(conv_ln_g[0])[:, :, 0], "ln_b": channels(conv_ln_b[0])[:, :, 0],
        "conv_proj": np.asarray(conv_proj_w)[0], "ret_proj": np.asarray(ret_proj_w)[0], "w_out": np.asarray(w_out)[0],
        "mix_g": np.asarray(norm_mix_g)[0], "ffn_g": np.asarray(norm_ffn_g)[0], "final_g": np.asarray(norm_final_g),
        "peer_wq": np.asarray(peer_w_q)[0],
        "keys": np.transpose(np.asarray(peer_sub_keys)[0].reshape(2 * PH, NK, P), (2, 0, 1)),
        "peer_u": np.asarray(peer_u)[0], "peer_v": np.asarray(peer_v)[0], **_tables(),
    }
    nc = bacc.Bacc("TRN2", target_bir_lowering=False, num_devices=1)
    arrays, args = {}, []
    for name in _NAMES:
        arrays[f"in_{name}"] = np.ascontiguousarray(given[name])
        args.append(nc.dram_tensor(f"in_{name}", arrays[f"in_{name}"].shape, f32, kind="ExternalInput").ap())
    out = nc.dram_tensor("out_y", (T, D), f32, kind="ExternalOutput").ap()
    block_kernel(nc, *args, out)
    result = run_bass_kernel_spmd(nc, [arrays], core_ids=[0])
    return result.results[0]["out_y"].reshape(1, T, D)
```
